# Optimizing a Trainium2 kernel written in Bass

```python
import jax, jax.numpy as jnp
from jax import lax
import numpy as np
import math

D_MODEL = 1024
BATCH = 1
SEQ = 512
DEPTH = 2

PLE_DIM = 256
HEAD_DIM = 64
SB_WIDTH = D_MODEL // 4
SB_HEADS = SB_WIDTH // HEAD_DIM
MLA_WIDTH = D_MODEL // 2
MLA_HEADS = MLA_WIDTH // HEAD_DIM
MLA_NOPE_DIM = 64
MLA_ROPE_DIM = 32
MLA_V_DIM = HEAD_DIM
MLA_Q_RANK = 384
MLA_KV_RANK = 256
CONV_WIDTH = D_MODEL // 4
CONV_K = 3
MIX_WIDTH = SB_WIDTH + MLA_WIDTH + CONV_WIDTH
IN_SIZES = (SB_WIDTH, SB_WIDTH, SB_WIDTH,
            MLA_Q_RANK, MLA_KV_RANK, MLA_ROPE_DIM,
            CONV_WIDTH, CONV_WIDTH, CONV_WIDTH)
IN_WIDTH = sum(IN_SIZES)
D_FF = 2816
Q_BLOCK = 128
ROPE_BASE = 10000.0
EPS = 1e-6
NEG_INF = -1e30


def rmsnorm(x, g):
    xf = x.astype(jnp.float32)
    y = xf * lax.rsqrt(jnp.mean(xf * xf, axis=-1, keepdims=True) + EPS)
    return (y * g.astype(jnp.float32)).astype(x.dtype)

def swiglu(x, w_gate, w_up, w_down):
    return (jax.nn.silu(x @ w_gate) * (x @ w_up)) @ w_down

def rope(x, pos):
    half = x.shape[-1] // 2
    inv = ROPE_BASE ** (-jnp.arange(half, dtype=jnp.float32) / half)
    ang = pos.astype(jnp.float32)[..., None] * inv
    cos = jnp.cos(ang)[:, :, None, :]
    sin = jnp.sin(ang)[:, :, None, :]
    xf = x.astype(jnp.float32)
    x1, x2 = xf[..., :half], xf[..., half:]
    return jnp.concatenate([x1 * cos - x2 * sin, x2 * cos + x1 * sin], axis=-1).astype(x.dtype)

def stick_breaking_attention(q, k, v):
    S = q.shape[1]
    scale = q.shape[-1] ** -0.5
    outs = []
    for start in range(0, S, Q_BLOCK):
        end = start + Q_BLOCK
        z = jnp.einsum("bqhd,bkhd->bhqk", q[:, start:end], k[:, :end],
                       preferred_element_type=jnp.float32) * scale
        t_idx = start + jnp.arange(Q_BLOCK)[:, None]
        s_idx = jnp.arange(end)[None, :]
        mask = s_idx < t_idx
        log_not = jnp.where(mask, -jax.nn.softplus(z), 0.0)
        after = lax.cumsum(log_not, axis=3, reverse=True) - log_not
        w = jnp.where(mask, jnp.exp(jax.nn.log_sigmoid(z) + after), 0.0)
        outs.append(jnp.einsum("bhqk,bkhd->bqhd", w.astype(v.dtype), v[:, :end]))
    return jnp.concatenate(outs, axis=1)

def latent_attention(c_q, c_kv, k_rope_raw, pos, g_q, g_kv, w_uq, w_ukv):
    B, S = c_q.shape[0], c_q.shape[1]
    q = (rmsnorm(c_q, g_q) @ w_uq).reshape(B, S, MLA_HEADS, MLA_NOPE_DIM + MLA_ROPE_DIM)
    q_nope, q_rope = q[..., :MLA_NOPE_DIM], rope(q[..., MLA_NOPE_DIM:], pos)
    kv = (rmsnorm(c_kv, g_kv) @ w_ukv).reshape(B, S, MLA_HEADS, MLA_NOPE_DIM + MLA_V_DIM)
    k_nope, v = kv[..., :MLA_NOPE_DIM], kv[..., MLA_NOPE_DIM:]
    k_rope = rope(k_rope_raw[:, :, None, :], pos)[:, :, 0, :]
    scale = (MLA_NOPE_DIM + MLA_ROPE_DIM) ** -0.5
    outs = []
    for start in range(0, S, Q_BLOCK):
        end = start + Q_BLOCK
        sc = (jnp.einsum("bqhd,bkhd->bhqk", q_nope[:, start:end], k_nope[:, :end],
                         preferred_element_type=jnp.float32)
              + jnp.einsum("bqhr,bkr->bhqk", q_rope[:, start:end], k_rope[:, :end],
                           preferred_element_type=jnp.float32)) * scale
        mask = jnp.arange(end)[None, :] <= (start + jnp.arange(Q_BLOCK)[:, None])
        w = jax.nn.softmax(jnp.where(mask, sc, NEG_INF), axis=-1)
        outs.append(jnp.einsum("bhqk,bkhd->bqhd", w.astype(v.dtype), v[:, :end]))
    return jnp.concatenate(outs, axis=1)

def short_gated_conv(b_gate, c_gate, h, w_conv):
    u = c_gate * h
    y = lax.conv_general_dilated(u, w_conv[:, None, :].astype(u.dtype), window_strides=(1,),
                                 padding=[(CONV_K - 1, 0)],
                                 dimension_numbers=("NWC", "WIO", "NWC"),
                                 feature_group_count=u.shape[-1])
    return b_gate * y

def first_inputs(seed: int = 0) -> dict:
    key = jax.random.key(seed)
    ks = iter(jax.random.split(key, 32))

    def dense(shape, fan_in):
        return jax.random.normal(next(ks), shape, jnp.float32) * fan_in ** -0.5

    def gain(dim):
        return 1.0 + 0.05 * jax.random.normal(next(ks), (DEPTH, dim), jnp.float32)

    x = jax.random.normal(next(ks), (BATCH, SEQ, D_MODEL), jnp.float32)
    p = jax.random.normal(next(ks), (DEPTH, BATCH, SEQ, PLE_DIM), jnp.float32)
    offsets = jax.random.randint(next(ks), (BATCH, 1), 0, 1024, dtype=jnp.int32)
    positions = offsets + jnp.arange(SEQ, dtype=jnp.int32)[None, :]
    return {
        "x": x, "p": p, "positions": positions,
        "g_ffn1_pre": gain(D_MODEL),
        "w1_gate": dense((DEPTH, D_MODEL, D_FF), D_MODEL),
        "w1_up": dense((DEPTH, D_MODEL, D_FF), D_MODEL),
        "w1_down": dense((DEPTH, D_FF, D_MODEL), D_FF),
        "g_ffn1_post": gain(D_MODEL),
        "g_mix_pre": gain(D_MODEL),
        "w_in": dense((DEPTH, D_MODEL, IN_WIDTH), D_MODEL),
        "g_mla_q": gain(MLA_Q_RANK),
        "w_mla_uq": dense((DEPTH, MLA_Q_RANK, MLA_HEADS * (MLA_NOPE_DIM + MLA_ROPE_DIM)), MLA_Q_RANK),
        "g_mla_kv": gain(MLA_KV_RANK),
        "w_mla_ukv": dense((DEPTH, MLA_KV_RANK, MLA_HEADS * (MLA_NOPE_DIM + MLA_V_DIM)), MLA_KV_RANK),
        "w_conv": dense((DEPTH, CONV_K, CONV_WIDTH), CONV_K),
        "w_out": dense((DEPTH, MIX_WIDTH, D_MODEL), MIX_WIDTH),
        "g_mix_post": gain(D_MODEL),
        "g_ffn2_pre": gain(D_MODEL),
        "w2_gate": dense((DEPTH, D_MODEL, D_FF), D_MODEL),
        "w2_up": dense((DEPTH, D_MODEL, D_FF), D_MODEL),
        "w2_down": dense((DEPTH, D_FF, D_MODEL), D_FF),
        "g_ffn2_post": gain(D_MODEL),
        "g_ple_pre": gain(D_MODEL),
        "w_ple_gate": dense((DEPTH, D_MODEL, D_MODEL), D_MODEL),
        "w_ple_proj": dense((DEPTH, PLE_DIM, D_MODEL), PLE_DIM),
        "g_ple_post": gain(D_MODEL),
    }

def first_block(x, p, positions, g_ffn1_pre, w1_gate, w1_up, w1_down, g_ffn1_post,
              g_mix_pre, w_in, g_mla_q, w_mla_uq, g_mla_kv, w_mla_ukv, w_conv, w_out,
              g_mix_post, g_ffn2_pre, w2_gate, w2_up, w2_down, g_ffn2_post,
              g_ple_pre, w_ple_gate, w_ple_proj, g_ple_post):
    B, S = x.shape[0], x.shape[1]
    split_at = [int(i) for i in np.cumsum(IN_SIZES)[:-1]]
    for i in range(DEPTH):
        h = rmsnorm(x, g_ffn1_pre[i])
        x = x + 0.5 * rmsnorm(swiglu(h, w1_gate[i], w1_up[i], w1_down[i]), g_ffn1_post[i])

        h = rmsnorm(x, g_mix_pre[i])
        (sb_q, sb_k, sb_v, c_q, c_kv, k_rope_raw,
         cv_b, cv_c, cv_h) = jnp.split(h @ w_in[i], split_at, axis=-1)
        heads = lambda t: t.reshape(B, S, SB_HEADS, HEAD_DIM)
        y_sb = stick_breaking_attention(heads(sb_q), heads(sb_k), heads(sb_v))
        y_mla = latent_attention(c_q, c_kv, k_rope_raw, positions, g_mla_q[i], g_mla_kv[i],
                                 w_mla_uq[i], w_mla_ukv[i])
        y_cv = short_gated_conv(cv_b, cv_c, cv_h, w_conv[i])
        mixed = jnp.concatenate([y_sb.reshape(B, S, SB_WIDTH),
                                 y_mla.reshape(B, S, MLA_WIDTH), y_cv], axis=-1) @ w_out[i]
        x = x + rmsnorm(mixed, g_mix_post[i])

        h = rmsnorm(x, g_ffn2_pre[i])
        x = x + 0.5 * rmsnorm(swiglu(h, w2_gate[i], w2_up[i], w2_down[i]), g_ffn2_post[i])

        h = rmsnorm(x, g_ple_pre[i])
        e = jax.nn.sigmoid(h @ w_ple_gate[i]) * (p[i].astype(x.dtype) @ w_ple_proj[i])
        x = x + rmsnorm(e, g_ple_post[i])
    return x


DEPTH_2 = 1

POOL_WINDOWS = (2, 4, 8, 16)
POOL_GROUPS = len(POOL_WINDOWS)
POOL_WIDTH = D_MODEL // 2
POOL_GROUP_DIM = POOL_WIDTH // POOL_GROUPS
RNN_WIDTH = D_MODEL
RNN_HEADS = 16
RNN_HEAD_DIM = RNN_WIDTH // RNN_HEADS
RNN_CONV = 4
LRU_C = 8.0
D_FF_2 = 3 * D_MODEL
FFN_CONV = 3
N_BRANCH = 2
RMS_EPS = 1e-6
IN_POOL = POOL_WIDTH
IN_RNN_X = RNN_WIDTH
IN_RNN_G = RNN_WIDTH
IN_GATES = N_BRANCH * D_MODEL
IN_TOTAL = IN_POOL + IN_RNN_X + IN_RNN_G + IN_GATES


def rms_norm(x, g):
    xf = x.astype(jnp.float32)
    y = xf * lax.rsqrt(jnp.mean(xf * xf, axis=-1, keepdims=True) + RMS_EPS) * g.astype(jnp.float32)
    return y.astype(x.dtype)

def causal_dwconv(u, w, b):
    k_w = w.shape[0]
    s = u.shape[1]
    up = jnp.pad(u, ((0, 0), (k_w - 1, 0), (0, 0)))
    out = b + up[:, 0:s] * w[0]
    for k in range(1, k_w):
        out = out + up[:, k:k + s] * w[k]
    return out

def pool_mixer(u, pool_w, pool_scale):
    b, s, _ = u.shape
    uf = u.astype(jnp.float32)
    cs = jnp.pad(jnp.cumsum(uf, axis=1), ((0, 0), (1, 0), (0, 0)))
    t = jnp.arange(s, dtype=jnp.int32)
    outs = []
    for g, w in enumerate(POOL_WINDOWS):
        sl = cs[..., g * POOL_GROUP_DIM:(g + 1) * POOL_GROUP_DIM]
        prev = jnp.pad(sl, ((0, 0), (w - 1, 0), (0, 0)))[:, :s]
        count = jnp.minimum(t + 1, w).astype(jnp.float32)[None, :, None]
        outs.append((sl[:, 1:] - prev) / count)
    mean = jnp.concatenate(outs, axis=-1)
    d = (mean - uf).astype(u.dtype).reshape(b, s, POOL_GROUPS, POOL_GROUP_DIM)
    y = jnp.einsum('bsgc,gcd->bsgd', d, pool_w).reshape(b, s, POOL_WIDTH)
    return y * pool_scale

def rg_lru_branch(xb, gb, conv_w, conv_b, w_gates, b_gates, lru_lambda):
    b, s, _ = xb.shape
    xc = causal_dwconv(xb, conv_w, conv_b)
    xh = xc.reshape(b, s, RNN_HEADS, RNN_HEAD_DIM)
    gates = jnp.einsum('bshi,ghij->gbshj', xh, w_gates).reshape(2, b, s, RNN_WIDTH)
    gates = gates.astype(jnp.float32) + b_gates.astype(jnp.float32)[:, None, None, :]
    r = jax.nn.sigmoid(gates[0])
    i = jax.nn.sigmoid(gates[1])
    log_a = -LRU_C * r * jax.nn.softplus(-lru_lambda.astype(jnp.float32))
    a = jnp.exp(log_a)
    mult = jnp.sqrt(-jnp.expm1(2.0 * log_a))
    t0 = (jnp.arange(s) == 0)[None, :, None]
    mult = jnp.where(t0, 1.0, mult)
    u = mult * i * xc.astype(jnp.float32)

    def combine(left, right):
        a_l, h_l = left
        a_r, h_r = right
        return a_l * a_r, a_r * h_l + h_r

    _, h = lax.associative_scan(combine, (a, u), axis=1)
    return h.astype(xb.dtype) * jax.nn.gelu(gb)

def second_inputs(seed: int = 0) -> dict:
    key = jax.random.key(seed)
    ks = jax.random.split(key, 32)
    f32 = jnp.float32
    L = DEPTH_2

    def nrm(k, shape, fan_in):
        return jax.random.normal(k, shape, f32) * (fan_in ** -0.5)

    def gain(k, shape):
        return 1.0 + 0.05 * jax.random.normal(k, shape, f32)

    a_c = jax.random.uniform(ks[10], (L, RNN_WIDTH), f32, 0.9, 0.999)
    s_l = a_c ** (1.0 / LRU_C)
    lru_lambda = jnp.log(s_l) - jnp.log1p(-s_l)

    return {
        "x": jax.random.normal(ks[0], (BATCH, SEQ, D_MODEL), f32),
        "p": jax.random.normal(ks[1], (DEPTH_2, BATCH, SEQ, PLE_DIM), f32),
        "g_mix_pre": gain(ks[2], (L, D_MODEL)),
        "g_mix_post": gain(ks[3], (L, D_MODEL)),
        "w_in": nrm(ks[4], (L, D_MODEL, IN_TOTAL), D_MODEL),
        "pool_w": nrm(ks[5], (L, POOL_GROUPS, POOL_GROUP_DIM, POOL_GROUP_DIM), POOL_GROUP_DIM),
        "pool_scale": gain(ks[6], (L, POOL_WIDTH)),
        "w_pool_out": nrm(ks[7], (L, POOL_WIDTH, D_MODEL), POOL_WIDTH),
        "conv_w": nrm(ks[8], (L, RNN_CONV, RNN_WIDTH), RNN_CONV),
        "conv_b": 0.02 * jax.random.normal(ks[9], (L, RNN_WIDTH), f32),
        "w_rg_gates": nrm(ks[11], (L, 2, RNN_HEADS, RNN_HEAD_DIM, RNN_HEAD_DIM), RNN_HEAD_DIM),
        "b_rg_gates": 0.02 * jax.random.normal(ks[12], (L, 2, RNN_WIDTH), f32),
        "lru_lambda": lru_lambda,
        "w_rg_out": nrm(ks[13], (L, RNN_WIDTH, D_MODEL), RNN_WIDTH),
        "w_o": nrm(ks[14], (L, D_MODEL, D_MODEL), D_MODEL),
        "g_ffn_pre": gain(ks[15], (L, D_MODEL)),
        "g_ffn_post": gain(ks[16], (L, D_MODEL)),
        "w_up": nrm(ks[17], (L, D_MODEL, 2 * D_FF_2), D_MODEL),
        "ffn_conv_w": nrm(ks[18], (L, FFN_CONV, D_FF_2), FFN_CONV),
        "ffn_conv_b": 0.02 * jax.random.normal(ks[19], (L, D_FF_2), f32),
        "w_down": nrm(ks[20], (L, D_FF_2, D_MODEL), D_FF_2),
        "g_ple_gate": gain(ks[21], (L, D_MODEL)),
        "w_ple_gate": nrm(ks[22], (L, D_MODEL, D_MODEL), D_MODEL),
        "w_ple_proj": nrm(ks[23], (L, PLE_DIM, D_MODEL), PLE_DIM),
        "g_ple_post": gain(ks[24], (L, D_MODEL)),
    }

def second_block(x, p, g_mix_pre, g_mix_post, w_in, pool_w, pool_scale, w_pool_out,
              conv_w, conv_b, w_rg_gates, b_rg_gates, lru_lambda, w_rg_out, w_o,
              g_ffn_pre, g_ffn_post, w_up, ffn_conv_w, ffn_conv_b, w_down,
              g_ple_gate, w_ple_gate, w_ple_proj, g_ple_post):
    for l in range(DEPTH_2):
        h = rms_norm(x, g_mix_pre[l])
        z = h @ w_in[l]
        c0 = IN_POOL
        c1 = c0 + IN_RNN_X
        c2 = c1 + IN_RNN_G
        u_pool = z[..., :c0]
        u_rx = z[..., c0:c1]
        u_rg = z[..., c1:c2]
        gate_pool = jax.nn.sigmoid(z[..., c2:c2 + D_MODEL])
        gate_rnn = jax.nn.sigmoid(z[..., c2 + D_MODEL:])

        y_pool = pool_mixer(u_pool, pool_w[l], pool_scale[l]) @ w_pool_out[l]
        y_rnn = rg_lru_branch(u_rx, u_rg, conv_w[l], conv_b[l], w_rg_gates[l],
                              b_rg_gates[l], lru_lambda[l]) @ w_rg_out[l]
        merged = gate_pool * y_pool + gate_rnn * y_rnn
        x = x + rms_norm(merged @ w_o[l], g_mix_post[l])

        h = rms_norm(x, g_ffn_pre[l])
        up = h @ w_up[l]
        gate_h = causal_dwconv(up[..., :D_FF_2], ffn_conv_w[l], ffn_conv_b[l])
        hid = jax.nn.gelu(gate_h) * up[..., D_FF_2:]
        x = x + rms_norm(hid @ w_down[l], g_ffn_post[l])

        ple_gate = jax.nn.sigmoid(rms_norm(x, g_ple_gate[l]) @ w_ple_gate[l])
        ple = rms_norm(p[l].astype(x.dtype) @ w_ple_proj[l], g_ple_post[l])
        x = x + ple_gate * ple
    return x


def setup_inputs(seed=0):
    out = dict(first_inputs(seed))
    for name, value in second_inputs(seed + 1).items():
        if name != "x":
            out[name + "_2"] = value
    return out


def reference(
    x, p, positions, g_ffn1_pre, w1_gate, w1_up, w1_down, g_ffn1_post, g_mix_pre, w_in, g_mla_q,
    w_mla_uq, g_mla_kv, w_mla_ukv, w_conv, w_out, g_mix_post, g_ffn2_pre, w2_gate, w2_up,
    w2_down, g_ffn2_post, g_ple_pre, w_ple_gate, w_ple_proj, g_ple_post, p_2, g_mix_pre_2,
    g_mix_post_2, w_in_2, pool_w_2, pool_scale_2, w_pool_out_2, conv_w_2, conv_b_2,
    w_rg_gates_2, b_rg_gates_2, lru_lambda_2, w_rg_out_2, w_o_2, g_ffn_pre_2, g_ffn_post_2,
    w_up_2, ffn_conv_w_2, ffn_conv_b_2, w_down_2, g_ple_gate_2, w_ple_gate_2, w_ple_proj_2,
    g_ple_post_2,
):
    x = first_block(
        x, p, positions, g_ffn1_pre, w1_gate, w1_up, w1_down, g_ffn1_post, g_mix_pre, w_in,
        g_mla_q, w_mla_uq, g_mla_kv, w_mla_ukv, w_conv, w_out, g_mix_post, g_ffn2_pre, w2_gate,
        w2_up, w2_down, g_ffn2_post, g_ple_pre, w_ple_gate, w_ple_proj, g_ple_post,
    )
    return second_block(
        x, p_2, g_mix_pre_2, g_mix_post_2, w_in_2, pool_w_2, pool_scale_2, w_pool_out_2,
        conv_w_2, conv_b_2, w_rg_gates_2, b_rg_gates_2, lru_lambda_2, w_rg_out_2, w_o_2,
        g_ffn_pre_2, g_ffn_post_2, w_up_2, ffn_conv_w_2, ffn_conv_b_2, w_down_2, g_ple_gate_2,
        w_ple_gate_2, w_ple_proj_2, g_ple_post_2,
    )


_drawn_inputs = setup_inputs


def setup_inputs(seed=0):
    import zlib

    import numpy as np

    out = dict(_drawn_inputs(seed))
    spreads = {}
    factors = {'g_mla_q': 7.43,
     'g_mla_kv': 4.621,
     'g_ffn2_post': 2.736,
     'g_ple_pre': 3.691,
     'g_mix_post_2': 2.882,
     'pool_scale_2': 3.359,
     'b_rg_gates_2': 50.554,
     'g_ffn_post_2': 3.14,
     'ffn_conv_b_2': 8.0,
     'g_ple_gate_2': 8.0,
     'g_ple_post_2': 6.029,
     'conv_b_2': 3.296}
    for name, (base, spread) in spreads.items():
        noise = np.random.default_rng([zlib.crc32(name.encode()), seed]).standard_normal(out[name].shape)
        drawn = base * np.exp(spread * noise) if base else spread * noise
        out[name] = __import__('jax').numpy.asarray(drawn.astype(out[name].dtype))
    for name, factor in factors.items():
        out[name] = (out[name] * factor).astype(out[name].dtype)
    return out
```

```python
from contextlib import ExitStack

import numpy as np

import concourse.bass as bass
from concourse import mybir

F32 = mybir.dt.float32
F32R = mybir.dt.float32r
I32 = mybir.dt.int32
ACT = mybir.ActivationFunctionType
ALU = mybir.AluOpType
AXX = mybir.AxisListType.X
ds = bass.ds

P = 128
T = 512
TC = T // P
D = 1024
DC = D // P
LAYERS = 2
FF = 2816
FF2 = 3072
EPS = 1e-6
NRAW = 2
NSPLIT = 4
UNIT = 1024
SEGS = 4
IN_W = 2208
SB_HEADS = 4
HD = 64
MLA_HEADS = 8
ROPE = 32
QK = HD + ROPE
Q_RANK = 384
PLE = 256
IN2 = 4608
LRU_C = 8.0
POOL_WINDOWS = (2, 4, 8, 16)
NEG_INF = -1e30
ROPE_BASE = 10000.0
CONSTS = 7 * P + HD + 1 + 16


class Sem:

    def __init__(self, handle):
        self.handle = handle
        self.levels = [0]


class Loop:

    def __init__(self, trips):
        self.trips = trips
        self.per_trip = {}


class Mark:

    def __init__(self, sem, levels, loops, back=0, off=0):
        self.sem, self.levels, self.loops, self.back, self.off = sem, levels, loops, back, off

    def prev(self):
        return Mark(self.sem, self.levels, self.loops, self.back + 1, self.off)

    def less(self, n):
        return Mark(self.sem, self.levels, self.loops, self.back, self.off - n)

    def value(self, regs):
        total = sum(self.levels) + self.off
        for n, loop in enumerate(self.loops):
            step = loop.per_trip.get(self.sem, 0)
            if not step:
                continue
            if n == len(self.loops) - 1:
                total = total - self.back * step
            if loop in regs:
                total = regs[loop] * step + total
            else:
                total = total + (loop.trips - 1) * step
        return total


class Program:

    ENGINES = ("sync", "scalar", "vector", "gpsimd", "tensor")

    def __init__(self):
        self.sems = []
        self.loops = []
        self.queues = {e: [[]] for e in self.ENGINES}

    def sem(self, handle):
        self.sems.append(Sem(handle))
        return self.sems[-1]

    def now(self, sem):
        return Mark(sem, list(sem.levels), list(self.loops))

    def put(self, engine, build, wait, sem, by):
        if sem is not None:
            sem.levels[-1] += by
        self.queues[engine][-1].append((build, [w for w in wait if w is not None], sem, by))
        return self.now(sem) if sem is not None else None

    def begin(self, trips):
        loop = Loop(trips)
        self.loops.append(loop)
        for s in self.sems:
            s.levels.append(0)
        for e in self.ENGINES:
            self.queues[e].append([])
        return loop

    def end(self):
        loop = self.loops.pop()
        for s in self.sems:
            body = s.levels.pop()
            loop.per_trip[s] = body
            s.levels[-1] += body * loop.trips
        for e in self.ENGINES:
            body = self.queues[e].pop()
            if body:
                self.queues[e][-1].append((loop, body))

    def emit(self, name, eng):
        self._emit(eng, self.queues[name][0], {})

    def _emit(self, eng, items, regs):
        for item in items:
            if len(item) == 2:
                loop, body = item
                with eng.Fori(0, loop.trips) as i:
                    self._emit(eng, body, {**regs, loop: i})
                continue
            build, wait, sem, by = item
            reg = lambda loop: regs[loop]
            if isinstance(build, tuple):
                build = build[0](eng, reg)
            latest, held = {}, []
            for w in wait:
                first = {loop: 0 for loop in regs}
                if w.sem not in latest or w.value(first) > latest[w.sem].value(first):
                    latest[w.sem] = w
            for w in latest.values():
                value = w.value(regs)
                if isinstance(value, int) and value <= 0:
                    continue
                if isinstance(item[0], tuple):
                    held.append((w.sem.handle, value if isinstance(value, int) else eng.to_reg(value)))
                else:
                    eng.wait_ge(w.sem.handle, value)
            ins = build(eng, reg)
            for handle, value in held:
                ins.wait_op(handle, value, "sem-ge")
            if sem is not None:
                ins.then_inc(sem.handle, by)


def split_kernel_params():
    layer = [("g_ffn1_pre", 8), ("g_ffn1_post", 8), ("g_mix_pre", 8), ("g_mla_q", 3), ("g_mla_kv", 2),
             ("w_conv", 6), ("g_mix_post", 8), ("g_ffn2_pre", 8), ("g_ffn2_post", 8), ("g_ple_pre", 8),
             ("g_ple_post", 8)]
    second = [[("g_mix_pre_2", 8), ("g_mix_post_2", 8), ("pool_scale_2", 4), ("conv_w_2", 32),
               ("conv_b_2", 8), ("b_rg_gates_2", 16), ("lru_lambda_2", 8), ("g_ffn_pre_2", 8)],
              [("g_ffn_post_2", 8), ("ffn_conv_w_2", 72), ("ffn_conv_b_2", 24), ("g_ple_gate_2", 8),
               ("g_ple_post_2", 8)]]
    return layer, second


def build_program(nc, a, consts_dram, out):
    pr = Program()
    with ExitStack() as ctx:
        def sem(name):
            return pr.sem(ctx.enter_context(nc.semaphore(name)))

        base = 16 * 1024 + 128
        KB = 1024
        cursor = [base]

        def take(size):
            at = cursor[0]
            cursor[0] += (size + 31) // 32 * 32
            assert cursor[0] <= nc.sbuf_usable_end, (cursor[0], nc.sbuf_usable_end)
            return at

        def at(name, shape, dt, offset):
            return nc.alloc_sbuf_tensor_at(name, shape, dt, offset=offset)

        def sb(name, shape, dt=F32):
            size = 4
            for s in shape[1:]:
                size *= s
            return at(name, shape, dt, take(size))

        X = sb("X", [P, DC, T])
        HH = sb("HH", [P, DC, T], F32R)
        HL = sb("HL", [P, DC, T], F32R)
        hid_at = take(96 * KB)
        raw = [sb(f"raw{i}", [P, UNIT]) for i in range(NRAW)]
        WH = [sb(f"WH{i}", [P, UNIT], F32R) for i in range(NSPLIT)]
        WL = [sb(f"WL{i}", [P, UNIT], F32R) for i in range(NSPLIT)]
        R = sb("R", [P, T])
        RP = sb("RP", [P, T])
        G = [sb(f"G{i}", [P, T]) for i in range(2)]
        U = [sb(f"U{i}", [P, T]) for i in range(2)]
        rope_at = take(4 * KB)
        consts = sb("consts", [P, CONSTS])
        par = sb("par", [P, 2 * 75 + 160 + 120])
        pcur = sb("pcur", [P, 75])
        eps = sb("eps", [P, 1])
        tiny = sb("tiny", [P, 1])
        first_means = sb("first_means", [P, 16])
        stats = sb("stats", [P, 12])
        masks = sb("masks", [P, 3, P], F32R)

        ident = consts[:, 0:P]
        ones = consts[:, P:2 * P]
        nones = consts[:, 2 * P:3 * P]
        ntri = consts[:, 3 * P:4 * P]
        mask01 = consts[:, 4 * P:5 * P]
        rot = consts[HD:HD + ROPE, 7 * P:7 * P + HD]
        inv_count = consts[:, 7 * P + HD + 1:7 * P + HD + 17]
        inv = consts[HD:HD + ROPE, 7 * P + HD:7 * P + HD + 1]
        identr, mask_sb, mask_mla = masks[:, 0, :], masks[:, 1, :], masks[:, 2, :]
        cosT = at("cosT", [P, T], F32, rope_at)
        sinT = at("sinT", [P, T], F32, rope_at + 2 * KB)

        HIDH = at("HIDH", [P, 24, T], F32R, hid_at)
        HIDL = at("HIDL", [P, 24, T], F32R, hid_at + 48 * KB)
        Y = at("Y", [P, DC, T], F32, hid_at)
        SQ = [G[0], G[1]]
        ACC = U[0]
        TMP = U[1]

        ps = [ctx.enter_context(nc.psum_tensor(f"ps{i}", [P, T], F32)) for i in range(8)]

        s_raw = [sem(f"s_raw{i}") for i in range(NRAW)]
        s_hi = sem("s_hi")
        s_lo = sem("s_lo")
        s_mm = sem("s_mm")
        s_t = sem("s_t")
        s_a = sem("s_a")
        s_d = sem("s_d")
        s_p = sem("s_p")
        s_par = sem("s_par")
        s_x = sem("s_x")
        s_pos = sem("s_pos")
        s_ptok = sem("s_ptok")
        s_misc = sem("s_misc")
        s_out = sem("s_out")
        n_fetch = pr.sem(None)
        n_used = pr.sem(None)

        def A(build, *wait):
            return pr.put("scalar", build, wait, s_a, 1)

        def V(build, *wait):
            return pr.put("vector", build, wait, s_d, 1)

        def G_(build, *wait):
            return pr.put("gpsimd", build, wait, s_p, 1)

        def TE(build, *wait):
            return pr.put("tensor", build, wait, s_t, 1)

        def mm(build, *wait):
            pr.put("tensor", build, wait, None, 0)

        def dma(build, s, *wait):
            return pr.put("sync", build, wait, s, 16)

        pr.put("sync", lambda e, r: e.sem_inc(s_lo.handle, NRAW), (), None, 0)
        pr.put("sync", lambda e, r: e.sem_inc(s_mm.handle, SEGS * NSPLIT), (), None, 0)
        s_lo.levels[0] = NRAW
        s_mm.levels[0] = SEGS * NSPLIT

        def fetch(parts):
            u = sum(n_fetch.levels)
            r, s = u % NRAW, u % NSPLIT
            slot_free = pr.now(s_lo).less(NRAW - 1)
            size = 0
            for src, shape in parts:
                n = 1
                for k in shape:
                    n *= k
                dst = raw[r][:, size:size + n]
                if len(shape) == 2:
                    dst = dst.rearrange("p (k n) -> p k n", k=shape[0])
                
                def prepare(e, reg, dst=dst, src=src):
                    weights = src(e, reg)
                    return lambda e, reg: e.dma_start(dst, weights)
                landed = dma((prepare,), s_raw[r], slot_free)
                size += n
            free = Mark(s_mm, [SEGS * c for c in n_fetch.levels], list(pr.loops), 0, SEGS)
            hi = pr.put("scalar", lambda e, reg: e.activation(WH[s][:, 0:size], raw[r][:, 0:size], ACT.Copy),
                        (landed, free), s_hi, 1)
            pr.put("vector", lambda e, reg: e.tensor_tensor(WL[s][:, 0:size], raw[r][:, 0:size],
                                                            WH[s][:, 0:size].bitcast(F32), ALU.subtract),
                   (hi,), s_lo, 1)
            n_fetch.levels[-1] += 1

        def use_unit(segments, first_waits=()):
            u = sum(n_used.levels)
            s = u % NSPLIT
            split = Mark(s_lo, list(n_used.levels), list(pr.loops), 0, NRAW + 1)
            wait0 = [split, *first_waits]
            ends = []
            assert len(segments) == SEGS
            for waits, tiles in segments:
                wait0 += waits
                for n, (o, w, ah, al, start, stop) in enumerate(tiles):
                    if w is None:
                        hi_, lo_ = ah
                        mh, ml = al(WH[s]), al(WL[s])
                        trio = [(hi_, mh), (lo_, mh), (hi_, ml)]
                    else:
                        wh, wl = w(WH[s]), w(WL[s])
                        trio = [(wh, ah), (wl, ah), (wh, al)]
                    for m, (lhs, rhs) in enumerate(trio):
                        last = n == len(tiles) - 1 and m == 2

                        def go(e, reg, o=o, lhs=lhs, rhs=rhs, st=start and m == 0, sp=stop and m == 2):
                            rr = rhs(reg) if callable(rhs) else rhs
                            return e.matmul(o, lhs, rr, start=st, stop=sp)
                        pr.put("tensor", go, wait0, s_mm if last else None, 1)
                        wait0 = []
                ends.append(pr.now(s_mm))
            n_used.levels[-1] += 1
            return ends

        def rows(name, first, k, col, width, layer=None, rows_per_layer=0):
            ap = a[name].rearrange("l k n -> (l k) n")

            def src(e, reg):
                f = first(reg) if callable(first) else first
                c = col(reg) if callable(col) else col
                if layer is not None:
                    f = reg(layer) * rows_per_layer + f
                f, c = [v if isinstance(v, int) else e.snap(v) for v in (f, c)]
                return ap[ds(f, k * P), ds(c, width)].rearrange("(k p) n -> p k n", p=P)
            return src

        sq_used = [None, None]
        first_sq = [None]
        acc_used = [None]

        def square_step(n, src, ready, *extra):
            b = n % 2
            q = A(lambda e, r: e.activation(SQ[b][:], src, ACT.Square), ready, sq_used[b], *extra)
            if n == 0:
                first_sq[0] = q
                return None
            if n == 1:
                p_ = G_(lambda e, r: e.tensor_tensor(ACC[:], SQ[0][:], SQ[1][:], ALU.add), first_sq[0], q,
                        acc_used[0], *extra)
                sq_used[0] = p_
            else:
                p_ = G_(lambda e, r: e.tensor_tensor(ACC[:], ACC[:], SQ[b][:], ALU.add), q, pr.now(s_p))
            sq_used[b] = p_
            return p_

        def prep_chunk(n, gain, ready, free):
            h = A(lambda e, r: e.activation(HH[:, n, :], X[:, n, :], ACT.Copy, scale=gain(n)), ready, *free)
            lo = V(lambda e, r: e.scalar_tensor_tensor(out=HL[:, n, :], in0=X[:, n, :], scalar=gain(n),
                                                       in1=HH[:, n, :].bitcast(F32), op0=ALU.mult,
                                                       op1=ALU.subtract), h)
            return lo

        def done():
            return [pr.now(s_t), pr.now(s_a), pr.now(s_d), pr.now(s_p)]

        c_in = dma(lambda e, r: e.dma_start(consts[:], consts_dram), s_par)
        xtok = at("xtok", [P, TC, D], F32, hid_at)
        x_in = [dma(lambda e, r, t=t: e.dma_start(xtok[:, t, :], a["x"][0, t * P:(t + 1) * P, :]), s_x)
                for t in range(TC)][-1]
        layer_rows, second_rows = split_kernel_params()
        ptile = at("ptile", [P, 4, P], F32, hid_at + 16 * KB)
        tiles = [[(n, k, l) for n, k in layer_rows] for l in range(LAYERS)]
        tiles += [[(n, k, 0) for n, k in part] for part in second_rows]
        cp, cs, widths = {}, {}, []
        for tno, part in enumerate(tiles):
            at_row = 0
            for name, k, l in part:
                src = a[name][l]
                src = (src.rearrange("(a r p) -> (a r) p", a=1, p=P) if len(src.shape) == 1
                       else src.rearrange("a (r p) -> (a r) p", p=P))
                par_in = dma(lambda e, r, tno=tno, q=at_row, k=k, src=src: e.dma_start(ptile[q:q + k, tno, :], src),
                             s_par)
                if tno < LAYERS:
                    cp[name] = at_row
                else:
                    cs[name] = sum(widths) + at_row
                at_row += k
            widths.append(at_row)
        posi = at("posi", [P, T], I32, hid_at + 18 * KB)
        pos_in = dma(lambda e, r: e.dma_start(posi[HD:HD + ROPE, :], a["positions"].to_broadcast([ROPE, T])), s_pos)

        V(lambda e, r: e.memset(eps[:], EPS))
        V(lambda e, r: e.memset(tiny[:], 1e-37))
        for i, c0 in enumerate((0, 5 * P, 6 * P)):
            A(lambda e, r, i=i, c0=c0: e.activation(masks[:, i, :], consts[:, c0:c0 + P], ACT.Copy), c_in, par_in)
        col = 0
        for tno, w in enumerate(widths):
            t = TE(lambda e, r, tno=tno, w=w: e.transpose(ps[tno][:, 0:w], ptile[0:w, tno, :], ident[0:w, 0:w]), par_in)
            V(lambda e, r, tno=tno, w=w, col=col: e.tensor_copy(par[:, col:col + w], ps[tno][:, 0:w]), t)
            col += w
        params = pr.now(s_d)
        for l in range(LAYERS):
            for name in ("g_ffn1_post", "g_ffn2_post"):
                c0 = l * widths[0] + cp[name]
                V(lambda e, r, c0=c0: e.tensor_scalar(par[:, c0:c0 + 8], par[:, c0:c0 + 8], 0.5, None, ALU.mult), params)

        x_done = []
        for n in range(DC):
            b = 4 + n % 4
            for t in range(TC):
                last = t == TC - 1
                (TE if last else mm)(
                    lambda e, r, n=n, t=t, b=b: e.transpose(ps[b][:, t * P:(t + 1) * P],
                                                            xtok[:, t, n * P:(n + 1) * P], ident),
                    x_in, c_in, *(x_done[n - 4:n - 3] if n >= 4 else ()))
            x_done.append(V(lambda e, r, n=n, b=b: e.tensor_copy(X[:, n, :], ps[b][:]), pr.now(s_t)))

        TWO_PI = 6.283185307179586
        C1 = 6.28125
        C2 = 0.0019350051879882812
        C3 = TWO_PI - C1 - C2
        MAGIC = 1.5 * 2.0 ** 23
        rows32 = slice(HD, HD + ROPE)
        ang = at("ang", [P, T], F32, hid_at + 20 * KB)
        turns = at("turns", [P, T], F32, hid_at + 22 * KB)
        m = V(lambda e, r: e.tensor_copy(ang[rows32, :], posi[rows32, :]), pos_in)
        m = V(lambda e, r: e.tensor_scalar(ang[rows32, :], ang[rows32, :], inv, None, ALU.mult), m, c_in, par_in)
        for table, quarter in ((sinT, 0.0), (cosT, 0.25)):
            m = V(lambda e, r, q=quarter: e.tensor_scalar(turns[rows32, :], ang[rows32, :], 1.0 / TWO_PI, q,
                                                          ALU.mult, ALU.add), m)
            m = V(lambda e, r: e.tensor_scalar(turns[rows32, :], turns[rows32, :], MAGIC, MAGIC, ALU.add,
                                               ALU.subtract), m)
            m = V(lambda e, r, t=table: e.scalar_tensor_tensor(out=t[rows32, :], in0=turns[rows32, :], scalar=-C1,
                                                               in1=ang[rows32, :], op0=ALU.mult, op1=ALU.add), m)
            for c in (-C2, -C3):
                m = V(lambda e, r, t=table, c=c: e.scalar_tensor_tensor(
                    out=t[rows32, :], in0=turns[rows32, :], scalar=c, in1=t[rows32, :], op0=ALU.mult, op1=ALU.add), m)
            m = V(lambda e, r, t=table, q=quarter: e.tensor_scalar(t[rows32, :], t[rows32, :], q * TWO_PI, 3.1415925,
                                                                   ALU.add, ALU.min), m)
            m = V(lambda e, r, t=table: e.tensor_scalar(t[rows32, :], t[rows32, :], -3.1415925, None, ALU.max), m)
            A(lambda e, r, t=table: e.activation(t[rows32, :], t[rows32, :], ACT.Sin), m)

        def prep(gain, x_ready, free, post=None, between=None):
            outs, sq = [], None
            for n in range(DC):
                ready = post(n) if post else x_ready[n]
                outs.append(prep_chunk(n, gain, ready, free))
                sq = square_step(n, X[:, n, :], ready)
                if between:
                    between(n)
            return outs, sq

        def group_unit(kcs, wat, banks, nk, act, waits_k, bank_waits):
            segs = []
            for bi, bank in enumerate(banks):
                tiles = [(ps[bank][:], (lambda W, j=j, bi=bi: wat(W, j, bi)), act[0][:, kc, :], act[1][:, kc, :],
                          kc == 0, kc == nk - 1) for j, kc in enumerate(kcs)]
                segs.append((list(bank_waits[bi] if kcs[0] == 0 else []) + (waits_k if bi == 0 else []), tiles))
            return segs

        def ev_waits():
            return [[pr.now(s_ev).less(3 - b)] for b in range(4)]

        def EV(build, *wait):
            return pr.put("vector", build, wait, s_ev, 1)

        def full_unit(kc, nk, act, waits, bank_waits, width=P, wcol=None):
            wcol = wcol or (lambda W, b: W[:, b * width:(b + 1) * width])
            segs = []
            for sgm in range(SEGS):
                tiles = []
                for b in (2 * sgm, 2 * sgm + 1):
                    tiles.append((ps[b][0:width, :], (lambda W, b=b: wcol(W, b)), act(kc)[0], act(kc)[1],
                                  kc == 0, kc == nk - 1))
                segs.append(((bank_waits[2 * sgm] + bank_waits[2 * sgm + 1] if kc == 0 else []) +
                             (waits if sgm == 0 else []), tiles))
            return segs

        HIDHf = HIDH[:, :, :].rearrange("p c t -> p (c t)")
        HIDLf = HIDL[:, :, :].rearrange("p c t -> p (c t)")

        def hid(k):
            if callable(k):
                return (lambda reg: HIDHf[:, ds(k(reg) * T, T)], lambda reg: HIDLf[:, ds(k(reg) * T, T)])
            return HIDH[:, k, :], HIDL[:, k, :]

        def down(n_hidden, n_peel, fetch_unit, next_units, early, late):
            free = [[pr.now(s_ev), *bank_free8] for b in range(8)]

            def one(k, kk, waits, ahead):
                segs = []
                for sgm in range(SEGS):
                    tiles = [(ps[b][:], (lambda W, b=b: W[:, b * P:(b + 1) * P]), hid(kk)[0], hid(kk)[1],
                              k == 0, k == n_hidden - 1) for b in (2 * sgm, 2 * sgm + 1)]
                    segs.append((free[2 * sgm] if k == 0 and sgm in (0, 2) else []) and
                                (free[2 * sgm] + (waits if sgm == 0 else []), tiles) or
                                ((waits if sgm == 0 else []), tiles))
                ends = use_unit(segs)
                ahead()
                return ends

            for k in range(n_peel):
                one(k, k, early if k == 0 else [], lambda: fetch(fetch_unit(k + NSPLIT)))
            trips = (n_hidden - NSPLIT - n_peel) // NSPLIT
            assert n_peel + NSPLIT * (trips + 1) == n_hidden
            loop = pr.begin(trips)
            for m_ in range(NSPLIT):
                k0 = n_peel + m_
                one(-1, lambda reg, k0=k0: reg(loop) * NSPLIT + k0, [],
                    lambda: fetch(fetch_unit(lambda reg, k0=k0: reg(loop) * NSPLIT + (k0 + NSPLIT))))
            pr.end()
            ends = None
            for m_ in range(NSPLIT):
                k = n_hidden - NSPLIT + m_
                last = m_ == NSPLIT - 1
                ends = one(k, k, late if k == n_hidden - 2 else [],
                           (lambda: None) if last else (lambda m_=m_: fetch(next_units[m_])))
            return ends

        def evacuate_y(ends):
            evs, sq = [], None
            for n in range(DC):
                ev = V(lambda e, r, n=n: e.tensor_copy(Y[:, n, :], ps[n][:]), ends[n // 2])
                evs.append(ev)
                sq = square_step(n, Y[:, n, :], ev)
            return evs, sq

        def update_x(gain, rp):
            def post(n):
                y = V(lambda e, r: e.scalar_tensor_tensor(out=Y[:, n, :], in0=Y[:, n, :], scalar=gain(n), in1=RP[:],
                                                          op0=ALU.mult, op1=ALU.mult), rp)
                return V(lambda e, r: e.tensor_tensor(X[:, n, :], X[:, n, :], Y[:, n, :], ALU.add), y)
            return post

        def rms(dst, bank, width, sq, *free):
            t = TE(lambda e, r: e.matmul(ps[bank][:], ones, ACC[:], start=True, stop=True), sq, *free)
            acc_used[0] = t
            ln = A(lambda e, r: e.activation(dst[:], ps[bank][:], ACT.Ln, bias=eps[:, 0:1], scale=1.0 / width), t)
            return A(lambda e, r: e.activation(dst[:], dst[:], ACT.Exp, scale=-0.5), ln)

        def swiglu_groups(h, sq, first_free, gate_up, n_groups, hidden_chunk, next_units, r_free):
            wat = lambda W, j, b: W[:, (b % 2) * 512 + j * 256 + (b // 2) * P:(b % 2) * 512 + j * 256 + (b // 2) * P + P]
            marks = []

            def one(g, first, ahead):
                r_m = None
                for kp in range(4):
                    waits_k = [h[2 * kp + 1]] if first else []
                    ends = use_unit(group_unit((2 * kp, 2 * kp + 1), wat, (0, 1, 2, 3), DC, (HH, HL), waits_k,
                                               first_free if first else ev_waits()))
                    if first and kp == 2:
                        r_m = rms(R, 7, D, sq, *r_free)
                    if kp < 3:
                        ahead(kp)
                hidden_chunk(g, ends, r_m, lambda: ahead(3))
                marks.append(pr.now(s_d))

            one(0, True, lambda kp: fetch(gate_up(1)[kp]))
            loop = pr.begin(n_groups - 2)
            gi = lambda reg: reg(loop) + 1
            one(gi, False, lambda kp: fetch(gate_up(lambda reg: reg(loop) + 2)[kp]))
            pr.end()
            body = marks[-1]
            one(n_groups - 1, False, lambda kp: fetch(next_units[kp]))
            return body, marks[-1]

        def gate_up_units(gate, up, up_col, layer):
            def units(g):
                col0 = (lambda reg: g(reg) * 256) if callable(g) else g * 256
                col1 = (lambda reg: g(reg) * 256 + up_col) if callable(g) else g * 256 + up_col
                return [[(rows(gate, kp * 256, 2, col0, 256, layer, D), (2, 256)),
                         (rows(up, kp * 256, 2, col1, 256, layer, D), (2, 256))] for kp in range(4)]
            return units

        def down_unit(name, n_rows, layer):
            def unit(k):
                first = (lambda reg: k(reg) * P) if callable(k) else k * P
                return [(rows(name, first, 1, 0, D, layer, n_rows), (1, D))]
            return unit

        def hid_slot(tile, g, j):
            return lambda reg: tile[:, ds((g(reg) * 2 + j) * T, T)] if callable(g) else tile[:, (g * 2 + j) * T:(g * 2 + j + 1) * T]

        def silu_chunk(g, ends, r_m, ahead):
            s_ = []
            for j in range(2):
                gm = EV(lambda e, r, j=j: e.tensor_tensor(G[j][:], ps[2 * j][:], R[:], ALU.mult), ends[2 * j], r_m)
                um = EV(lambda e, r, j=j: e.tensor_tensor(U[j][:], ps[2 * j + 1][:], R[:], ALU.mult), ends[2 * j + 1])
                s_.append((A(lambda e, r, j=j: e.activation(G[j][:], G[j][:], ACT.Silu), gm), um))
            ahead()
            fs = [V(lambda e, r, j=j: e.tensor_tensor(U[j][:], U[j][:], G[j][:], ALU.mult), *s_[j]) for j in range(2)]
            for j in range(2):
                hh = A(lambda e, r, j=j: e.activation(hid_slot(HIDHf, g, j)(r), U[j][:], ACT.Copy), fs[j])
                V(lambda e, r, j=j: e.tensor_tensor(hid_slot(HIDLf, g, j)(r), U[j][:],
                                                    hid_slot(HIDHf, g, j)(r).bitcast(F32), ALU.subtract), hh)

        PTOK = at("PTOK", [P, TC, PLE], F32, hid_at + 44 * KB)
        PTL = at("PTL", [P, 2, T], F32R, hid_at + 44 * KB)
        PTH = at("PTH", [P, 2, T], F32R, hid_at + 92 * KB)
        E = at("E", [P, DC, T], F32, hid_at + 16 * KB)
        wat4 = lambda W, j, b: W[:, j * 512 + b * P:j * 512 + b * P + P]

        def embeddings(landed, bank, free):
            for c in range(2):
                for t in range(TC):
                    (TE if t == TC - 1 else mm)(
                        lambda e, r, c=c, t=t: e.transpose(ps[bank + c][:, t * P:(t + 1) * P],
                                                           PTOK[:, t, c * P:(c + 1) * P], ident), landed, *free)
            t_ = pr.now(s_t)
            for c in range(2):
                hh = A(lambda e, r, c=c: e.activation(PTH[:, c, :], ps[bank + c][:], ACT.Copy), t_)
                V(lambda e, r, c=c: e.tensor_tensor(PTL[:, c, :], ps[bank + c][:], PTH[:, c, :].bitcast(F32),
                                                    ALU.subtract), hh)

        def ple_units(proj, gate, layer):
            col = lambda name, k, c: [(rows(name, k * P, 2, c, 512, layer, a[name].shape[1]), (2, 512))]
            return [col(proj, 0, c) for c in (0, 512)], [col(gate, 2 * kp, c) for c in (0, 512) for kp in range(4)]

        def embedding_products(free, ahead, b0, waits=()):
            pt = pr.now(s_d) if b0 == 0 else None
            e_ = use_unit([([*waits, *free[b0 + b:b0 + b + 1], pt],
                            [(ps[b0 + b][:], (lambda W, j=j, b=b: wat4(W, j, b)), PTH[:, j, :], PTL[:, j, :],
                              j == 0, j == 1) for j in range(2)]) for b in range(TC)])
            fetch(ahead[0])
            return [A(lambda e, r, b=b: e.activation(E[:, b0 + b, :], ps[b0 + b][:], ACT.Copy), e_[b])
                    for b in range(TC)]

        pcol = lambda name: (lambda n, c=cp[name]: pcur[:, c + n:c + n + 1])
        scol = lambda name: (lambda n, c=cs[name]: par[:, c + n:c + n + 1])
        s_ev = sem("s_ev")
        bank_free8 = []

        ready0 = done()
        layer = pr.begin(LAYERS)
        start = done()
        pc = V(lambda e, r: e.tensor_copy(pcur[:], par[:, ds(r(layer) * widths[0], widths[0])]), *ready0, *start)

        gu1 = gate_up_units("w1_gate", "w1_up", 0, layer)
        dn1 = down_unit("w1_down", FF, layer)
        for kp in range(4):
            fetch(gu1(0)[kp])
        h, sq = prep(pcol("g_ffn1_pre"), [pc] * DC, start)
        early, late = swiglu_groups(h, sq, [start] * 4, gu1, FF // 256, silu_chunk, [dn1(k) for k in range(4)], start)
        win_units = [[(rows("w_in", kp * 256, 2, c, 512, layer, D), (2, 512))] for c in (512, 1024, 0, 1440)
                     for kp in range(4)]
        win_units += [[(rows("w_in", kp * 256, 2, 1952, 256, layer, D), (2, 256))] for kp in range(4)]
        ends = down(FF // P, 2, dn1, win_units, [early], [late])
        evs, sq = evacuate_y(ends)
        rp = rms(RP, 4, D, sq, evs[4])
        free = [evs[b:b + 1] for b in range(4)]
        h, sq = prep(pcol("g_mix_pre"), None, [], post=update_x(pcol("g_ffn1_post"), rp))
        fetch(win_units[3])

        def mixer_tile(name, shape, kb, dt=F32):
            return at(name, shape, dt, hid_at + int(kb * KB))

        QS = mixer_tile("QS", [P, 2, T], 0)
        KS = mixer_tile("KS", [P, 2, T], 4)
        VS = mixer_tile("VS", [P, TC, 256], 8)
        QM = mixer_tile("QM", [P, MLA_HEADS, T], 12)
        KM = mixer_tile("KM", [P, MLA_HEADS, T], 28)
        VF = mixer_tile("VF", [P, 2, T], 28)
        VM = mixer_tile("VM", [P, TC, 512], 44)
        KR = mixer_tile("KR", [P, T], 52)
        CQ = mixer_tile("CQ", [P, 5, T], 54)
        CH = mixer_tile("CH", [P, 5, T], 64, F32R)
        CL = mixer_tile("CL", [P, 5, T], 74, F32R)
        CV = mixer_tile("CV", [P, 6, T], 84)
        PB = [mixer_tile(f"PB{i}", [P, T], 54 + 2 * i) for i in range(4)]
        PT = [mixer_tile(f"PT{i}", [P, TC, T], 62 + 8 * i) for i in range(2)]
        SP = mixer_tile("SP", [P, TC, T], 78)
        SW = mixer_tile("SW", [P, TC, T], 86)

        wat = lambda W, j, b: W[:, j * 512 + b * P:j * 512 + b * P + P]

        def win_group(first, ahead, w=wat, banks=(0, 1, 2, 3)):
            r_m = None
            for kp in range(4):
                waits_k = [h[2 * kp + 1]] if first else []
                segs = group_unit((2 * kp, 2 * kp + 1), w, banks, DC, (HH, HL), waits_k, free if first else ev_waits())
                while len(segs) < SEGS:
                    segs = [(w_, [t]) for w_, ts in segs for t in (ts[0], ts[1])]
                    for i_ in (1, 3):
                        segs[i_] = ([], segs[i_][1])
                e_ = use_unit(segs)
                if first and kp == 2:
                    r_m = rms(R, 7, D, sq, evs[7])
                fetch(ahead[kp])
            return e_, r_m

        def take_r(dst, bank, end, *wait):
            return EV(lambda e, r: e.tensor_tensor(dst, ps[bank][:], R[:], ALU.mult), end, *wait)

        ends, r_m = win_group(True, win_units[4:8])
        vf = [take_r(VF[:, j, :], j, ends[j], r_m) for j in range(2)]
        cq = [take_r(CQ[:, j, :], 2 + j, ends[2 + j]) for j in range(2)]
        wr = lambda W, j, b: W[:, j * 512 + (b * P if b < 3 else 320):j * 512 + (b * P if b < 3 else 320) + P]
        ends, _ = win_group(False, win_units[8:12], wr)
        cq += [take_r(CQ[:, 2 + j, :], j, ends[j]) for j in range(3)]
        kr = EV(lambda e, r: e.tensor_tensor(KR[rows32, :], ps[3][rows32, :], R[rows32, :], ALU.mult), ends[3])
        vs = None
        for j in range(2):
            for t in range(TC):
                (TE if t == TC - 1 else mm)(
                    lambda e, r, j=j, t=t: e.transpose(ps[4 + j][:, t * P:(t + 1) * P],
                                                       VF[:, j, t * P:(t + 1) * P], ident), vf[1])
            vs = V(lambda e, r, j=j: e.tensor_copy(
                VS[:, :, j * P:(j + 1) * P], ps[4 + j][:].rearrange("p (t c) -> p t c", t=TC)), pr.now(s_t))
        krot = TE(lambda e, r: e.matmul(ps[6][HD:P, :], rot, KR[rows32, :], start=True, stop=True), kr)

        def rope(dst, bank, rotated):
            m1 = V(lambda e, r: e.tensor_tensor(G[0][rows32, :], ps[bank][rows32, :], sinT[rows32, :], ALU.mult),
                   rotated, pr.now(s_d))
            m2 = V(lambda e, r: e.tensor_tensor(dst, dst, cosT[rows32, :], ALU.mult), rotated)
            return V(lambda e, r: e.tensor_tensor(dst, dst, G[0][rows32, :], ALU.add), m1, m2)

        def latent_norm(dst, chunks, width, bank, gain, c0):
            sq_ = None
            for n, c in enumerate(chunks):
                sq_ = square_step(n, CQ[:, c, :], cq[c], r_m)
            rq = rms(dst, bank, width, sq_)
            for n, c in enumerate(chunks):
                m1 = V(lambda e, r, c=c, n=n: e.scalar_tensor_tensor(
                    out=CQ[:, c, :], in0=CQ[:, c, :], scalar=gain(n), in1=dst[:], op0=ALU.mult, op1=ALU.mult), rq)
                hh = A(lambda e, r, c=c: e.activation(CH[:, c, :], CQ[:, c, :], ACT.Copy), m1)
                out_ = V(lambda e, r, c=c: e.tensor_tensor(CL[:, c, :], CQ[:, c, :], CH[:, c, :].bitcast(F32),
                                                           ALU.subtract), hh)
            return out_

        ends, _ = win_group(False, win_units[12:16])
        qs = [EV(lambda e, r, j=j: e.scalar_tensor_tensor(out=QS[:, j, :], in0=ps[j][:], scalar=HD ** -0.5,
                                                          in1=R[:], op0=ALU.mult, op1=ALU.mult), ends[j])
              for j in range(2)]
        ks = [take_r(KS[:, j, :], 2 + j, ends[2 + j]) for j in range(2)]
        cqn = latent_norm(RP, (0, 1, 2), Q_RANK, 5, pcol("g_mla_q"), 0)
        ckvn = latent_norm(U[1], (3, 4), PLE, 4, pcol("g_mla_kv"), 3)
        kr = rope(KR[rows32, :], 6, krot)
        ends, _ = win_group(False, win_units[16:20])
        cv = [take_r(CV[:, j, :], j, ends[j]) for j in range(4)]
        wh_ = lambda W, j, b: W[:, j * 256 + b * P:j * 256 + b * P + P]
        uq = [[(rows("w_mla_uq", k * P, 1, 0, 768, layer, Q_RANK), (1, 768))] for k in range(3)]
        ukv = [[(rows("w_mla_ukv", k * P, 1, 0, 1024, layer, PLE), (1, 1024))] for k in range(2)]
        def value_cols(k):
            ap = a["w_mla_ukv"].rearrange("l k (h c) -> (l k) h c", h=MLA_HEADS)

            def src(e, reg):
                return ap[ds(e.snap(reg(layer) * PLE + k * P), P), :, HD:2 * HD]
            return src
        lat_units = uq + ukv + [[(value_cols(k), (MLA_HEADS, HD)) for k in range(2)]]
        ends, _ = win_group(False, lat_units[0:4], wh_, banks=(0, 1))
        cv += [take_r(CV[:, 4 + j, :], j, ends[2 * j + 1]) for j in range(2)]

        win_done = pr.now(s_mm)
        wc = lambda k, j: pcur[:, cp["w_conv"] + 2 * k + j:cp["w_conv"] + 2 * k + j + 1]
        for j in range(2):
            u_ = V(lambda e, r, j=j: e.tensor_tensor(CV[:, 2 + j, :], CV[:, 2 + j, :], CV[:, 4 + j, :], ALU.mult),
                   cv[4 + j])
            y_ = V(lambda e, r, j=j: e.tensor_scalar(CV[:, 4 + j, :], CV[:, 2 + j, :], wc(2, j), None, ALU.mult), u_)
            for k, sh in ((1, 1), (0, 2)):
                y_ = V(lambda e, r, j=j, k=k, sh=sh: e.scalar_tensor_tensor(
                    out=CV[:, 4 + j, sh:T], in0=CV[:, 2 + j, 0:T - sh], scalar=wc(k, j), in1=CV[:, 4 + j, sh:T],
                    op0=ALU.mult, op1=ALU.add), y_)
            y_ = V(lambda e, r, j=j: e.tensor_tensor(CV[:, 4 + j, :], CV[:, 4 + j, :], CV[:, j, :], ALU.mult), y_)
            hh = A(lambda e, r, j=j: e.activation(HH[:, 6 + j, :], CV[:, 4 + j, :], ACT.Copy), y_, win_done)
            conv_done = V(lambda e, r, j=j: e.tensor_tensor(HL[:, 6 + j, :], CV[:, 4 + j, :],
                                                            HH[:, 6 + j, :].bitcast(F32), ALU.subtract), hh)

        chl = lambda c0: (lambda kc: (CH[:, c0 + kc, :], CL[:, c0 + kc, :]))
        bw = [[cv[4], cv[5]]] * 2 + [[cv[2], cv[3]]] * 2 + [[ckvn], [cqn], [kr], [kr]]
        out_units = [[(rows("w_out", k * P, 1, 0, D, layer, D), (1, D))] for k in range(8)]
        nxt = lat_units[4:6] + out_units[0:4]

        for k in range(3):
            ends = use_unit(full_unit(k, 3, chl(0), [cqn], bw, width=QK))
            fetch(nxt[k])
        qm = []
        for hd in range(MLA_HEADS):
            q_ = A(lambda e, r, hd=hd: e.activation(QM[0:QK, hd, :], ps[hd][0:QK, :], ACT.Copy, scale=QK ** -0.5),
                   ends[hd // 2])
            qm.append(q_)
        for k in range(2):
            ends = use_unit(full_unit(k, 2, chl(3), [], [[q_] for q_ in qm]))
            fetch(nxt[3 + k])
        km = []
        for hd in range(MLA_HEADS):
            k_ = V(lambda e, r, hd=hd: e.tensor_copy(KM[0:HD, hd, :], ps[hd][0:HD, :]), ends[hd // 2], vs)
            k2 = V(lambda e, r, hd=hd: e.tensor_copy(KM[rows32, hd, :], KR[rows32, :]), kr, vs)
            km.append([k_, k2])
        segs = []
        for t in range(TC):
            sl = slice(t * P, (t + 1) * P)
            segs.append(([km[t][0]],
                         [(ps[t][:], None, (CH[:, 3 + k, sl], CL[:, 3 + k, sl]),
                           (lambda W, k=k: W[:, k * 512:(k + 1) * 512]), k == 0, k == 1) for k in range(2)]))
        ends = use_unit(segs)
        fetch(nxt[5])
        vm = [A(lambda e, r, t=t: e.activation(VM[:, t, :], ps[t][:], ACT.Copy), ends[t]) for t in range(TC)]
        qrot = []
        for hd in range(MLA_HEADS):
            b = 4 + hd % 4
            t_ = TE(lambda e, r, hd=hd, b=b: e.matmul(ps[b][HD:P, :], rot, QM[rows32, hd, :], start=True, stop=True),
                    qm[hd], km[b][0], *(qrot[hd - 4:hd - 3] if hd >= 4 else []))
            qrot.append(rope(QM[rows32, hd, :], b, t_))
        lat_in = [qrot[-1], vm[-1], km[-1][1]]
        sc_read, tp_read, pb_read = [None] * 2, [None] * 2, [None] * 4
        pt_read, pv_read = [None] * 2, [None] * 2
        scored = {}

        def lat_score(n):
            hd, i, b = n // TC, n % TC, n % 2
            w_ = (i + 1) * P
            mm(lambda e, r: e.matmul(ps[b][:, 0:w_], QM[0:QK, hd, i * P:w_], KM[0:QK, hd, 0:w_],
                                     start=True, stop=False), *(lat_in if n < 2 else []), sc_read[b])
            scored[n] = TE(lambda e, r: e.matmul(ps[b][:, i * P:w_], identr, mask_mla, start=False, stop=True))

        def lat_softmax(n):
            i, b, c = n % TC, n % 2, n % 4
            w_ = (i + 1) * P
            nm, rs, ri = stats[:, c:c + 1], stats[:, 4 + c:5 + c], stats[:, 8 + c:9 + c]
            m_ = V(lambda e, r: e.tensor_reduce(out=nm, in_=ps[b][:, 0:w_], axis=AXX, op=ALU.max, negate=True),
                   scored[n], pb_read[c])
            x_ = A(lambda e, r: e.activation(PB[c][:, 0:w_], ps[b][:, 0:w_], ACT.Exp, bias=nm, accum_out=rs),
                   m_, pb_read[c])
            sc_read[b] = x_
            d_ = V(lambda e, r: e.reciprocal(ri, rs), x_)
            return V(lambda e, r: e.tensor_scalar(PB[c][:, 0:w_], PB[c][:, 0:w_], ri, None, ALU.mult), d_)

        def lat_transpose(n, p_):
            hd, i, b, c = n // TC, n % TC, 2 + n % 2, n % 4
            for j in range(i + 1):
                (TE if j == i else mm)(lambda e, r, j=j: e.transpose(
                    ps[b][:, j * P:(j + 1) * P], PB[c][:, j * P:(j + 1) * P], ident), p_, tp_read[b - 2])
            t_ = pr.now(s_t)
            pb_read[c] = t_
            tp_read[b - 2] = V(lambda e, r: e.tensor_copy(
                PT[hd % 2][:, 0:i + 1, i * P:(i + 1) * P],
                ps[b][:, 0:(i + 1) * P].rearrange("p (j c) -> p j c", j=i + 1)), t_, pt_read[hd % 2])
            return tp_read[b - 2]

        def values(hd, bank, vals, weights, ready, chunk):
            rr = slice((hd % 2) * HD, (hd % 2) * HD + HD)
            for j in range(TC):
                (TE if j == TC - 1 else mm)(lambda e, r, j=j: e.matmul(
                    ps[bank][rr, j * P:T], vals[:, j, hd * HD:(hd + 1) * HD], weights[:, j, j * P:T],
                    start=j == 0, stop=j == TC - 1), *(ready if j == 0 else []), pv_read[bank - 6])
            t_ = pr.now(s_t)
            hh = A(lambda e, r: e.activation(HH[rr, chunk, :], ps[bank][rr, :], ACT.Copy), t_, win_done)
            pv_read[bank - 6] = V(lambda e, r: e.tensor_tensor(
                HL[rr, chunk, :], ps[bank][rr, :], HH[rr, chunk, :].bitcast(F32), ALU.subtract), hh)
            return t_

        z_read, acc_read, sp_read, sw_read = [None], [None], [None], [None]
        T1 = (G[0], G[1])
        t1_free = [pr.now(s_d)] * 2

        def sb_z(m, start_, bank, wait):
            hd, j = m // TC, TC - 1 - m % TC
            rr = slice((hd % 2) * HD, (hd % 2) * HD + HD)
            return TE(lambda e, r: e.matmul(ps[bank][:, j * P:T], KS[rr, hd // 2, j * P:(j + 1) * P],
                                            QS[rr, hd // 2, j * P:T], start=True, stop=start_), *wait)

        def sb_softplus(m, z_):
            j, b = TC - 1 - m % TC, m % 2
            t1 = T1[b][:, j * P:T]
            x_ = A(lambda e, r: e.activation(t1, ps[4][:, j * P:T], ACT.Abs), z_, t1_free[b])
            x_ = A(lambda e, r: e.activation(t1, t1, ACT.Exp, scale=-1.0), x_)
            x_ = A(lambda e, r: e.activation(t1, t1, ACT.Ln, bias=1.0), x_)
            d_ = V(lambda e, r: e.scalar_tensor_tensor(out=SP[:, j, j * P:T], in0=ps[4][:, j * P:T], scalar=0.0,
                                                       in1=t1, op0=ALU.max, op1=ALU.add), x_, sp_read[0])
            z_read[0] = t1_free[b] = d_
            return V(lambda e, r: e.tensor_tensor(SP[:, j, j * P:(j + 1) * P], SP[:, j, j * P:(j + 1) * P],
                                                  mask01, ALU.mult), d_)

        def sb_weights(m, sp_):
            j = TC - 1 - m % TC
            sb_z(m, False, 5, [sp_, acc_read[0]])
            mm(lambda e, r: e.matmul(ps[5][:, j * P:T], ntri, SP[:, j, j * P:T], start=False, stop=False))
            for j2 in range(j + 1, TC):
                mm(lambda e, r, j2=j2: e.matmul(ps[5][:, j2 * P:T], nones, SP[:, j2, j2 * P:T],
                                                start=False, stop=False))
            t_ = TE(lambda e, r: e.matmul(ps[5][:, j * P:(j + 1) * P], identr, mask_sb, start=False, stop=True))
            if j == 0:
                sp_read[0] = t_
            acc_read[0] = A(lambda e, r: e.activation(SW[:, j, j * P:T], ps[5][:, j * P:T], ACT.Exp), t_,
                            sw_read[0])
            return acc_read[0]

        lat_score(0)
        z_m = sb_z(0, True, 4, [qrot[-1], ks[1]])
        lat_score(1)
        for rnd in range(16):
            soft = [lat_softmax(2 * rnd)]
            sp_ = sb_softplus(rnd, z_m)
            soft.append(lat_softmax(2 * rnd + 1))
            if rnd < 15:
                lat_score(2 * rnd + 2)
                z_m = sb_z(rnd + 1, True, 4, [z_read[0]])
            lat_transpose(2 * rnd, soft[0])
            w_m = sb_weights(rnd, sp_)
            if rnd < 15:
                lat_score(2 * rnd + 3)
            tp = lat_transpose(2 * rnd + 1, soft[1])
            if rnd % 2 == 1:
                hd = rnd // 2
                pt_read[hd % 2] = values(hd, 6, VM, PT[hd % 2], [tp], 2 + hd // 2)
            if rnd % 4 == 3:
                sw_read[0] = values(rnd // 4, 7, VS, SW, [w_m], rnd // 8)
        mixed = [pv_read[0], pv_read[1], conv_done]

        gu2 = gate_up_units("w2_gate", "w2_up", 0, layer)
        dn2 = down_unit("w2_down", FF, layer)
        bank_w = [[acc_read[0], tp_read[0], tp_read[1], sc_read[0], sc_read[1], z_read[0]]] + [[]] * 5 + [mixed] * 2
        for k in range(8):
            ends = use_unit(full_unit(k, 8, lambda kc: (HH[:, kc, :], HL[:, kc, :]), mixed if k == 0 else [],
                                      bank_w))
            if k < 4:
                fetch(out_units[4 + k])
            elif k < 7:
                fetch(gu2(0)[k - 4])
        p_in = dma((lambda e, reg: (lambda src: (lambda e, reg: e.dma_start(PTOK[:], src)))(
            a["p"].rearrange("l b (t q) c -> (l b) q t c", q=P)[ds(e.snap(reg(layer) * 1), 1), :, :, :]
            .rearrange("l q t c -> (l q) t c")),), s_ptok, pv_read[0], pv_read[1])
        evs, sq = evacuate_y(ends)
        rp = rms(RP, 4, D, sq, evs[4])
        free = [evs[b:b + 1] for b in range(4)]
        h, sq = prep(pcol("g_ffn2_pre"), None, [], post=update_x(pcol("g_mix_post"), rp))
        fetch(gu2(0)[3])
        embeddings(p_in, 5, evs[5:8])
        early, late = swiglu_groups(h, sq, free, gu2, FF // 256, silu_chunk,
                                    [dn2(k) for k in range(4)], [evs[7]])
        pproj, gates = ple_units("w_ple_proj", "w_ple_gate", layer)
        ple_u = pproj + gates
        ends = down(FF // P, 2, dn2, ple_u[0:4], [early], [late])
        evs, sq = evacuate_y(ends)
        fetch(ple_u[3])
        eb = embedding_products(evs, ple_u[4:5], 0)
        rp = rms(RP, 4, D, sq, evs[4])
        eb += embedding_products(evs, ple_u[5:6], 4, [rp])
        h, sq = prep(pcol("g_ple_pre"), None, [], post=update_x(pcol("g_ffn2_post"), rp))
        sq = None
        for half in range(2):
            for kp in range(4):
                e_ = use_unit(group_unit((2 * kp, 2 * kp + 1), wat4, range(4 * half, 4 * half + 4), DC, (HH, HL),
                                         [h[2 * kp + 1]] if half == 0 else [], [[m_] for m_ in eb[4 * half:4 * half + 4]]
                                         if half == 0 else [[eb[b], r_m] for b in range(4, 8)]))
                if half == 0 and kp == 2:
                    r_m = rms(R, 7, D, pr.now(s_p), eb[7])
                if half == 0 and kp < 4 and 4 * half + kp + 6 < len(ple_u):
                    fetch(ple_u[4 * half + kp + 6])
            for q in range(4):
                n = 4 * half + q
                z_ = V(lambda e, r, n=n: e.tensor_tensor(Y[:, n, :], ps[n][:], R[:], ALU.mult), e_[q], r_m)
                z_ = A(lambda e, r, n=n: e.activation(Y[:, n, :], Y[:, n, :], ACT.Sigmoid), z_)
                z_ = V(lambda e, r, n=n: e.tensor_tensor(Y[:, n, :], Y[:, n, :], E[:, n, :], ALU.mult), z_)
                sq = square_step(n, Y[:, n, :], z_)
        rp = rms(RP, 0, D, sq)
        for n in range(DC):
            update_x(pcol("g_ple_post"), rp)(n)
        pr.end()
        start = done()
        LX = at("LX", [P, DC, T], F32, hid_at)
        LXH = at("LXH", [P, DC, T], F32R, hid_at)
        XC = at("XC", [P, DC, T], F32, hid_at + 16 * KB)
        UP = at("UP", [P, TC, T], F32, hid_at + 32 * KB)
        UPL = at("UPL", [P, TC, T], F32R, hid_at + 32 * KB)
        LG = at("LG", [P, DC, T], F32, hid_at + 40 * KB)
        LGL = at("LGL", [P, DC, T], F32R, hid_at + 40 * KB)
        GP = at("GP", [P, DC, T], F32, hid_at + 56 * KB)
        TH = at("TH", [P, DC, T], F32, hid_at + 72 * KB)
        GR = at("GR", [P, DC, T], F32, hid_at + 72 * KB)
        PH = at("PH", [P, TC, T], F32R, hid_at + 88 * KB)
        bd = at("bd", [P, 16, P], F32, hid_at + 88 * KB)
        pw = at("pw", [P, TC, P], F32, rope_at)
        lam = at("lam", [P, 3, 8], F32, rope_at + 2 * KB)

        win2 = lambda c: [[(rows("w_in_2", kp * 256, 2, c, 512), (2, 512))] for kp in range(4)]
        w2 = [u for c in (512, 1024, 0, 1536, 2048, 2560, 3072, 3584, 4096) for u in win2(c)]
        w2 += [[(rows("w_pool_out_2", k * P, 1, 0, D), (1, D))] for k in range(4)]
        w2 += [[(rows(w, k * P, 1, 0, D), (1, D))] for w in ("w_rg_out_2", "w_o_2") for k in range(8)]
        gu = gate_up_units("w_up_2", "w_up_2", FF2, None)
        w2 += gu(0)
        at_unit = [0]

        def ahead():
            fetch(w2[at_unit[0]])
            at_unit[0] += 1

        pw_in = dma(lambda e, r: e.dma_start(pw[:], a["pool_w_2"][0].rearrange("g c d -> c g d")), s_par, *start)
        for _ in range(NSPLIT):
            ahead()
        bd0 = G_(lambda e, r: e.memset(bd[:], 0.0), *start)
        heads = a["w_rg_gates_2"].rearrange("l g (h q) i j -> q i (l g h) j", q=2)
        bd_in = [dma(lambda e, r, q=q: e.dma_start(bd[q * HD:(q + 1) * HD, :, q * HD:(q + 1) * HD], heads[q]), s_par, bd0)
                 for q in range(2)][-1]
        h, sq = prep(scol("g_mix_pre_2"), [start[2]] * DC, start)
        lm = par[:, cs["lru_lambda_2"]:cs["lru_lambda_2"] + 8]
        l_ = A(lambda e, r: e.activation(lam[:, 2, :], lm, ACT.Abs), *start)
        l_ = A(lambda e, r: e.activation(lam[:, 2, :], lam[:, 2, :], ACT.Exp, scale=-1.0), l_)
        l_ = A(lambda e, r: e.activation(lam[:, 2, :], lam[:, 2, :], ACT.Ln, bias=1.0), l_)
        m_ = V(lambda e, r: e.tensor_scalar(lam[:, 0, :], lm, -1.0, 0.0, ALU.mult, ALU.max), *start)
        m_ = V(lambda e, r: e.tensor_tensor(lam[:, 0, :], lam[:, 0, :], lam[:, 2, :], ALU.add), l_, m_)
        l_ = V(lambda e, r: e.tensor_scalar(lam[:, 1, :], lam[:, 0, :], -LRU_C, None, ALU.mult), m_)
        lam_done = V(lambda e, r: e.tensor_scalar(lam[:, 0, :], lam[:, 0, :], LRU_C, None, ALU.mult), l_)

        def in_group(no):
            r_m = None
            for kp in range(4):
                ends = use_unit(group_unit((2 * kp, 2 * kp + 1), wat4, (0, 1, 2, 3), DC, (HH, HL),
                                           [h[2 * kp + 1]] if no == 0 else [],
                                           [start] * 4 if no == 0 else ev_waits()))
                if no == 0 and kp == 2:
                    r_m = rms(R, 7, D, sq, *start)
                ahead()
            return ends, r_m

        def take4(dst, c0, ends, r_m=None):
            return [EV(lambda e, r, j=j: e.tensor_tensor(dst[:, c0 + j, :], ps[j][:], R[:], ALU.mult), ends[j], r_m)
                    for j in range(4)]

        ends, r_m = in_group(0)
        lx = take4(LX, 0, ends, r_m)
        ends, _ = in_group(1)
        lx += take4(LX, 4, ends)
        ends, _ = in_group(2)
        up = take4(UP, 0, ends)
        sq_sum = pr.now(s_t)

        xc = []

        def conv4(n):
            cw = lambda k: par[:, cs["conv_w_2"] + 8 * k + n:cs["conv_w_2"] + 8 * k + n + 1]
            y_ = V(lambda e, r: e.tensor_scalar(XC[:, n, :], LX[:, n, :], cw(3), scol("conv_b_2")(n), ALU.mult,
                                                ALU.add), lx[n])
            for k, sh in ((2, 1), (1, 2), (0, 3)):
                y_ = V(lambda e, r, k=k, sh=sh: e.scalar_tensor_tensor(
                    out=XC[:, n, sh:T], in0=LX[:, n, 0:T - sh], scalar=cw(k), in1=XC[:, n, sh:T],
                    op0=ALU.mult, op1=ALU.add), y_)
            xc.append(y_)

        gate_read = {}
        scan_in, tanh_done, r_done = [], [], []
        tmp_read = [pr.now(s_p)] * 2

        def lru_gates(n):
            br, bi = 4 + 2 * (n % 2), 5 + 2 * (n % 2)
            tr = TE(lambda e, r: e.matmul(ps[br][:], bd[:, n, :], XC[:, n, :], start=True, stop=True),
                    xc[n], bd_in, r_m, *gate_read.get(br, []))
            ti = TE(lambda e, r: e.matmul(ps[bi][:], bd[:, 8 + n, :], XC[:, n, :], start=True, stop=True),
                    *gate_read.get(bi, []))
            rg = A(lambda e, r: e.activation(LX[:, n, :], ps[br][:], ACT.Sigmoid, bias=scol("b_rg_gates_2")(n)), tr)
            ig = A(lambda e, r: e.activation(G[n % 2][:], ps[bi][:], ACT.Sigmoid, bias=scol("b_rg_gates_2")(8 + n)),
                   ti, tmp_read[n % 2])
            gate_read[br], gate_read[bi] = [rg], [ig]
            r_done.append(rg)
            tanh_done.append(A(lambda e, r: e.activation(TH[:, n, :], LX[:, n, :], ACT.Tanh,
                                                         scale=lam[:, 0, n:n + 1]), rg, lam_done))
            s_ = V(lambda e, r: e.tensor_tensor(XC[:, n, :], XC[:, n, :], G[n % 2][:], ALU.mult), ig)
            tmp_read[n % 2] = s_
            scan_in.append(s_)

        pool_d = []
        scratch = (U[0], U[1])
        for g, width in enumerate(POOL_WINDOWS):
            src, m_ = UP[:, g, :], up[g]
            step, side = 1, 0
            while step < width:
                dst = scratch[side]
                m1 = G_(lambda e, r, d=dst, s_=src, k=step: e.tensor_tensor(d[:, k:T], s_[:, k:T], s_[:, 0:T - k],
                                                                           ALU.add), m_, sq_sum, *pool_d[-1:])
                m_ = G_(lambda e, r, d=dst, s_=src, k=step: e.tensor_copy(d[:, 0:k], s_[:, 0:k]), m1)
                src, step, side = dst, 2 * step, 1 - side
            m_ = V(lambda e, r, s_=src, w=width: e.tensor_tensor(first_means[:, 0:w], s_[:, 0:w], inv_count[:, 0:w],
                                                                 ALU.mult), m_, *pool_d[-1:])
            m1 = V(lambda e, r, s_=src, w=width, g=g: e.scalar_tensor_tensor(
                out=UP[:, g, w:T], in0=s_[:, w:T], scalar=1.0 / w, in1=UP[:, g, w:T], op0=ALU.mult,
                op1=ALU.subtract), m_)
            pool_d.append(V(lambda e, r, w=width, g=g: e.tensor_tensor(UP[:, g, 0:w], first_means[:, 0:w],
                                                                       UP[:, g, 0:w], ALU.subtract), m1))

        for n in range(4):
            conv4(n)
        for no in (3, 4):
            ends, _ = in_group(no)
            lg = take4(LG, 4 * (no - 3), ends)
            for n in range(4 * (no - 3), 4 * (no - 3) + 4):
                lru_gates(n)
            if no == 3:
                for n in range(4, 8):
                    conv4(n)
        bd_read = pr.now(s_t)
        ph = []
        for g in range(4):
            t_ = TE(lambda e, r, g=g: e.matmul(ps[4 + g][:], pw[:, g, :], UP[:, g, :], start=True, stop=True),
                    pool_d[g], pw_in, gate_read[4 + g][0])
            hh = A(lambda e, r, g=g: e.activation(PH[:, g, :], ps[4 + g][:], ACT.Copy, scale=scol("pool_scale_2")(g)),
                   t_, bd_read)
            ph.append(V(lambda e, r, g=g: e.scalar_tensor_tensor(
                out=UPL[:, g, :], in0=ps[4 + g][:], scalar=scol("pool_scale_2")(g), in1=PH[:, g, :].bitcast(F32),
                op0=ALU.mult, op1=ALU.subtract), hh))
        gp = []
        for no in (5, 6):
            ends, _ = in_group(no)
            c0 = 4 * (no - 5)
            g_ = take4(GP, c0, ends)
            gp += [A(lambda e, r, c=c0 + j: e.activation(GP[:, c, :], GP[:, c, :], ACT.Sigmoid), g_[j]) for j in range(4)]
        mults = []
        for n in range(DC):
            b = n % 2
            a_ = A(lambda e, r, n=n: e.activation(LX[:, n, :], LX[:, n, :], ACT.Exp, scale=lam[:, 1, n:n + 1]),
                   tanh_done[n])
            l1 = A(lambda e, r, n=n, b=b: e.activation(G[b][:], TH[:, n, :], ACT.Ln, bias=1.0), tanh_done[n], tmp_read[b])
            l2 = A(lambda e, r, n=n: e.activation(TH[:, n, :], TH[:, n, :], ACT.Ln, scale=2.0, bias=tiny[:, 0:1]), l1)
            d_ = V(lambda e, r, n=n, b=b: e.tensor_tensor(TH[:, n, :], TH[:, n, :], G[b][:], ALU.subtract), l2)
            tmp_read[b] = d_
            m_ = A(lambda e, r, n=n: e.activation(TH[:, n, :], TH[:, n, :], ACT.Exp, scale=0.5), d_)
            m_ = V(lambda e, r, n=n: e.memset(TH[:, n, 0:1], 1.0), m_)
            m_ = V(lambda e, r, n=n: e.tensor_tensor(XC[:, n, :], XC[:, n, :], TH[:, n, :], ALU.mult), m_, scan_in[n])
            mults.append(V(lambda e, r, n=n: e.tensor_tensor_scan(XC[:, n, :], LX[:, n, :], XC[:, n, :], 0.0,
                                                                  ALU.mult, ALU.add), m_, a_))
        gr = []
        for no in (7, 8):
            ends, _ = in_group(no)
            c0 = 4 * (no - 7)
            g_ = [EV(lambda e, r, c=c0 + j, j=j: e.tensor_tensor(GR[:, c, :], ps[j][:], R[:], ALU.mult), ends[j],
                     mults[-1]) for j in range(4)]
            gr += [A(lambda e, r, c=c0 + j: e.activation(GR[:, c, :], GR[:, c, :], ACT.Sigmoid), g_[j]) for j in range(4)]
        for n in range(DC):
            g_ = A(lambda e, r, n=n: e.activation(LG[:, n, :], LG[:, n, :], ACT.Gelu_apprx_tanh), lg[3])
            m_ = V(lambda e, r, n=n: e.tensor_tensor(XC[:, n, :], XC[:, n, :], LG[:, n, :], ALU.mult), g_, mults[n])
            hh = A(lambda e, r, n=n: e.activation(LXH[:, n, :], XC[:, n, :], ACT.Copy), m_)
            lo = V(lambda e, r, n=n: e.tensor_tensor(LGL[:, n, :], XC[:, n, :], LXH[:, n, :].bitcast(F32),
                                                     ALU.subtract), hh)
            mults[n] = lo
        for k in range(4):
            ends = use_unit(full_unit(k, 4, lambda kc: (PH[:, kc, :], UPL[:, kc, :]), [ph[k]],
                                      [w_ for w_ in ev_waits()] + [[ph[b]] for b in range(4)]))
            ahead()
        in_read = pr.now(s_mm)
        yp = [V(lambda e, r, n=n: e.tensor_tensor(GP[:, n, :], GP[:, n, :], ps[n][:], ALU.mult), ends[n // 2], gp[n])
              for n in range(DC)]
        for k in range(8):
            ends = use_unit(full_unit(k, 8, lambda kc: (LXH[:, kc, :], LGL[:, kc, :]), [mults[k]], [[y_] for y_ in yp]))
            ahead()
        mh, yr = [], []
        for n in range(DC):
            y_ = V(lambda e, r, n=n: e.tensor_tensor(GR[:, n, :], GR[:, n, :], ps[n][:], ALU.mult), ends[n // 2], gr[n])
            yr.append([y_])
            m_ = V(lambda e, r, n=n: e.tensor_tensor(GR[:, n, :], GR[:, n, :], GP[:, n, :], ALU.add), y_, yp[n])
            hh = A(lambda e, r, n=n: e.activation(HH[:, n, :], GR[:, n, :], ACT.Copy), m_, in_read)
            mh.append(V(lambda e, r, n=n: e.tensor_tensor(HL[:, n, :], GR[:, n, :], HH[:, n, :].bitcast(F32),
                                                          ALU.subtract), hh))
        for k in range(8):
            ends = use_unit(full_unit(k, 8, lambda kc: (HH[:, kc, :], HL[:, kc, :]), [mh[k]], yr))
            if k < 7:
                ahead()
        evs, sq = evacuate_y(ends)
        rp = rms(RP, 4, D, sq, evs[4])
        free = [evs[b:b + 1] for b in range(4)]

        h, sq = prep(scol("g_ffn_pre_2"), None, [], post=update_x(scol("g_mix_post_2"), rp))
        ahead()
        CG = [at(f"CG{j}", [P, T], F32, rope_at + 2 * KB * j) for j in range(2)]
        fw_cols = sb("fw_cols", [P, 4, 2])
        cw0, cb0 = cs["ffn_conv_w_2"], cs["ffn_conv_b_2"]
        taps = par[:, cw0:cw0 + 72].rearrange("p (k c) -> p k c", k=3)

        def conv_gelu_chunk(g, ends, r_m, ahead):
            dyn = lambda r: ds(g(r) * 2, 2) if callable(g) else slice(2 * g, 2 * g + 2)
            dynb = lambda r: ds(g(r) * 2 + cb0, 2) if callable(g) else slice(cb0 + 2 * g, cb0 + 2 * g + 2)
            V(lambda e, r: e.tensor_copy(fw_cols[:, 0:3, :], taps[:, :, dyn(r)]), pr.now(s_d))
            V(lambda e, r: e.tensor_copy(fw_cols[:, 3, :], par[:, dynb(r)]), pr.now(s_d))
            s_ = []
            for j in range(2):
                gm = EV(lambda e, r, j=j: e.tensor_tensor(G[j][:], ps[2 * j][:], R[:], ALU.mult), ends[2 * j], r_m)
                um = EV(lambda e, r, j=j: e.tensor_tensor(U[j][:], ps[2 * j + 1][:], R[:], ALU.mult), ends[2 * j + 1])
                c_ = V(lambda e, r, j=j: e.tensor_scalar(CG[j][:], G[j][:], fw_cols[:, 2, j:j + 1],
                                                         fw_cols[:, 3, j:j + 1], ALU.mult, ALU.add), gm, pr.now(s_d))
                for k, sh in ((1, 1), (0, 2)):
                    c_ = V(lambda e, r, j=j, k=k, sh=sh: e.scalar_tensor_tensor(
                        out=CG[j][:, sh:T], in0=G[j][:, 0:T - sh], scalar=fw_cols[:, k, j:j + 1],
                        in1=CG[j][:, sh:T], op0=ALU.mult, op1=ALU.add), c_)
                s_.append((A(lambda e, r, j=j: e.activation(CG[j][:], CG[j][:], ACT.Gelu_apprx_tanh), c_), um))
            ahead()
            fs = [V(lambda e, r, j=j: e.tensor_tensor(U[j][:], U[j][:], CG[j][:], ALU.mult), *s_[j]) for j in range(2)]
            for j in range(2):
                hh = A(lambda e, r, j=j: e.activation(hid_slot(HIDHf, g, j)(r), U[j][:], ACT.Copy), fs[j])
                V(lambda e, r, j=j: e.tensor_tensor(hid_slot(HIDLf, g, j)(r), U[j][:],
                                                    hid_slot(HIDHf, g, j)(r).bitcast(F32), ALU.subtract), hh)

        dn = down_unit("w_down_2", FF2, None)
        early, late = swiglu_groups(h, sq, free, gu, FF2 // 256, conv_gelu_chunk, [dn(k) for k in range(4)],
                                    [evs[7]])
        pproj, gates = ple_units("w_ple_proj_2", "w_ple_gate_2", None)
        ple_u = pproj + gates
        ends = down(FF2 // P, 4, dn, ple_u[0:4], [early], [late])
        p_in = dma(lambda e, r: e.dma_start(PTOK[:], a["p_2"][0, 0].rearrange("(t q) c -> q t c", q=P)), s_ptok,
                   ends[3])
        evs, sq = evacuate_y(ends)
        fetch(ple_u[3])
        rp = rms(RP, 4, D, sq, evs[4])
        embeddings(p_in, 5, evs[5:7])
        eb = embedding_products(evs, ple_u[4:5], 0)
        eb += embedding_products(evs, ple_u[5:6], 4, [rp, pr.now(s_a), pr.now(s_d)])
        h, sq = prep(scol("g_ple_gate_2"), None, [], post=update_x(scol("g_ffn_post_2"), rp))
        for half in range(2):
            for kp in range(4):
                e_ = use_unit(group_unit((2 * kp, 2 * kp + 1), wat4, range(4 * half, 4 * half + 4), DC, (HH, HL),
                                         [h[2 * kp + 1]] if half == 0 else [],
                                         [[m_] for m_ in eb[0:4]] if half == 0 else [[eb[b], r_m] for b in range(4, 8)]))
                if half == 0 and kp == 2:
                    r_m = rms(R, 7, D, sq, eb[7])
                    for n in range(DC):
                        sq = square_step(n, E[:, n, :], eb[n], r_m)
                if half == 0:
                    fetch(ple_u[kp + 6])
                if half == 1 and kp == 1:
                    re = rms(U[1], 0, D, sq, z0)
                    for n in range(DC):
                        V(lambda e, r, n=n: e.scalar_tensor_tensor(out=E[:, n, :], in0=E[:, n, :],
                                                                   scalar=scol("g_ple_post_2")(n), in1=U[1][:],
                                                                   op0=ALU.mult, op1=ALU.mult), re)
                    en = pr.now(s_d)
            for q in range(4):
                n = 4 * half + q
                z_ = V(lambda e, r, n=n: e.tensor_tensor(Y[:, n, :], ps[n][:], R[:], ALU.mult), e_[q], r_m)
                if n == 0:
                    z0 = z_
                z_ = A(lambda e, r, n=n: e.activation(Y[:, n, :], Y[:, n, :], ACT.Sigmoid), z_)
                if half == 1:
                    for c in ([n - 4, n] if True else []):
                        y_ = V(lambda e, r, c=c: e.tensor_tensor(Y[:, c, :], Y[:, c, :], E[:, c, :], ALU.mult), z_, en)
                        V(lambda e, r, c=c: e.tensor_tensor(X[:, c, :], X[:, c, :], Y[:, c, :], ALU.add), y_)
        fin = done()
        otok = at("otok", [P, TC, D], F32, hid_at + 24 * KB)
        o_evs = []
        for t in range(TC):
            for half in range(2):
                b = (t * 2 + half) % 4
                for q in range(4):
                    n = half * 4 + q
                    (TE if q == 3 else mm)(
                        lambda e, r, b=b, q=q, n=n, t=t: e.transpose(ps[b][:, q * P:(q + 1) * P],
                                                                     X[:, n, t * P:(t + 1) * P], ident),
                        *(fin if q == 0 and not o_evs else []), *(o_evs[-4:-3] if len(o_evs) >= 4 else []))
                o_evs.append(V(lambda e, r, b=b, t=t, half=half: e.tensor_copy(
                    otok[:, t, half * 512:(half + 1) * 512], ps[b][:]), pr.now(s_t)))
            dma(lambda e, r, t=t: e.dma_start(out[0, t * P:(t + 1) * P, :], otok[:, t, :]), s_out, o_evs[-1])
        all_out = pr.now(s_out)

        block = ctx.enter_context(nc.Block())

        @block.sync
        def _(e):
            pr.emit("sync", e)
            e.wait_ge(s_out.handle, all_out.value({}))

        @block.scalar
        def _(e):
            pr.emit("scalar", e)

        @block.vector
        def _(e):
            pr.emit("vector", e)

        @block.gpsimd
        def _(e):
            pr.emit("gpsimd", e)

        @block.tensor
        def _(e):
            pr.emit("tensor", e)


INPUTS = ("x", "p", "positions", "g_ffn1_pre", "w1_gate", "w1_up", "w1_down", "g_ffn1_post", "g_mix_pre", "w_in",
          "g_mla_q", "w_mla_uq", "g_mla_kv", "w_mla_ukv", "w_conv", "w_out", "g_mix_post", "g_ffn2_pre", "w2_gate",
          "w2_up", "w2_down", "g_ffn2_post", "g_ple_pre", "w_ple_gate", "w_ple_proj", "g_ple_post", "p_2",
          "g_mix_pre_2", "g_mix_post_2", "w_in_2", "pool_w_2", "pool_scale_2", "w_pool_out_2", "conv_w_2", "conv_b_2",
          "w_rg_gates_2", "b_rg_gates_2", "lru_lambda_2", "w_rg_out_2", "w_o_2", "g_ffn_pre_2", "g_ffn_post_2",
          "w_up_2", "ffn_conv_w_2", "ffn_conv_b_2", "w_down_2", "g_ple_gate_2", "w_ple_gate_2", "w_ple_proj_2",
          "g_ple_post_2")


def constant_table():
    row, col = np.arange(P)[:, None], np.arange(P)[None, :]
    c = np.zeros((P, CONSTS), np.float32)
    c[:, 0:P] = row == col
    c[:, P:2 * P] = 1
    c[:, 2 * P:3 * P] = -1
    c[:, 3 * P:4 * P] = np.where(row >= col, -1, 0)
    c[:, 4 * P:5 * P] = row < col
    c[:, 5 * P:6 * P] = np.where(row < col, 0, NEG_INF)
    c[:, 6 * P:7 * P] = np.where(col <= row, 0, NEG_INF)
    half = ROPE // 2
    for m in range(half):
        c[HD + m + half, 7 * P + m] = -1
        c[HD + m, 7 * P + half + m] = 1
    freq = np.float32(ROPE_BASE) ** (-np.arange(half, dtype=np.float32) / np.float32(half))
    c[HD:HD + half, 7 * P + HD] = c[HD + half:HD + ROPE, 7 * P + HD] = freq
    c[:, 7 * P + HD + 1:] = 1.0 / np.arange(1, 17, dtype=np.float32)
    return c


def kernel(**inputs):
    import concourse.bacc as bacc
    from concourse.bass_utils import run_bass_kernel_spmd

    nc = bacc.Bacc("TRN2", target_bir_lowering=False, num_devices=1)
    arrays, aps = {}, {}
    for name in INPUTS:
        v = np.ascontiguousarray(inputs[name])
        arrays[f"in_{name}"] = v
        aps[name] = nc.dram_tensor(f"in_{name}", v.shape, mybir.dt.from_np(v.dtype), kind="ExternalInput").ap()
    arrays["in_constants"] = constant_table()
    consts_dram = nc.dram_tensor("in_constants", (P, CONSTS), F32, kind="ExternalInput").ap()
    out = nc.dram_tensor("out_x", (1, T, D), F32, kind="ExternalOutput").ap()
    build_program(nc, aps, consts_dram, out)
    return run_bass_kernel_spmd(nc, [arrays], core_ids=[0]).results[0]["out_x"]
```

```python
from contextlib import ExitStack

import numpy as np

import concourse.bass as bass
from concourse import mybir

F32 = mybir.dt.float32
F32R = mybir.dt.float32r
I32 = mybir.dt.int32
ACT = mybir.ActivationFunctionType
ALU = mybir.AluOpType
AXX = mybir.AxisListType.X
ds = bass.ds

P = 128
T = 512
TC = T // P
D = 1024
DC = D // P
LAYERS = 2
FF = 2816
FF2 = 3072
EPS = 1e-6
NRAW = 2
NSPLIT = 4
UNIT = 1024
SEGS = 4
SB_HEADS = 4
HD = 64
MLA_HEADS = 8
ROPE = 32
QK = HD + ROPE
Q_RANK = 384
PLE = 256
LRU_C = 8.0
POOL_WINDOWS = (2, 4, 8, 16)
NEG_INF = -1e30
ROPE_BASE = 10000.0
CONSTS = 8 * P + 1 + 16


class Sem:

    def __init__(self, handle):
        self.handle = handle
        self.levels = [0]


class Loop:

    def __init__(self, trips):
        self.trips = trips
        self.per_trip = {}


class Mark:

    def __init__(self, sem, levels, loops, off=0):
        self.sem, self.levels, self.loops, self.off = sem, levels, loops, off

    def less(self, n):
        return Mark(self.sem, self.levels, self.loops, self.off - n)

    def value(self, regs):
        total = sum(self.levels) + self.off
        for loop in self.loops:
            step = loop.per_trip.get(self.sem, 0)
            if not step:
                continue
            if loop in regs:
                total = regs[loop] * step + total
            else:
                total = total + (loop.trips - 1) * step
        return total


class Program:

    ENGINES = ("sync", "scalar", "vector", "gpsimd", "tensor")

    def __init__(self):
        self.sems = []
        self.loops = []
        self.queues = {e: [[]] for e in self.ENGINES}

    def sem(self, handle):
        self.sems.append(Sem(handle))
        return self.sems[-1]

    def now(self, sem):
        return Mark(sem, list(sem.levels), list(self.loops))

    def put(self, engine, build, wait, sem, by):
        if sem is not None:
            sem.levels[-1] += by
        self.queues[engine][-1].append((build, [w for w in wait if w is not None], sem, by))
        return self.now(sem) if sem is not None else None

    def begin(self, trips):
        loop = Loop(trips)
        self.loops.append(loop)
        for s in self.sems:
            s.levels.append(0)
        for e in self.ENGINES:
            self.queues[e].append([])
        return loop

    def end(self):
        loop = self.loops.pop()
        for s in self.sems:
            body = s.levels.pop()
            loop.per_trip[s] = body
            s.levels[-1] += body * loop.trips
        for e in self.ENGINES:
            body = self.queues[e].pop()
            if body:
                self.queues[e][-1].append((loop, body))

    def emit(self, name, eng):
        self._emit(eng, self.queues[name][0], {})

    def _emit(self, eng, items, regs):
        for item in items:
            if len(item) == 2:
                loop, body = item
                with eng.Fori(0, loop.trips) as i:
                    self._emit(eng, body, {**regs, loop: i})
                continue
            build, wait, sem, by = item
            reg = lambda loop: regs[loop]
            if isinstance(build, tuple):
                build = build[0](eng, reg)
            latest, held = {}, []
            for w in wait:
                first = {loop: 0 for loop in regs}
                if w.sem not in latest or w.value(first) > latest[w.sem].value(first):
                    latest[w.sem] = w
            for w in latest.values():
                value = w.value(regs)
                if isinstance(value, int) and value <= 0:
                    continue
                if isinstance(item[0], tuple):
                    held.append((w.sem.handle, value if isinstance(value, int) else eng.to_reg(value)))
                else:
                    eng.wait_ge(w.sem.handle, value)
            ins = build(eng, reg)
            for handle, value in held:
                ins.wait_op(handle, value, "sem-ge")
            if sem is not None:
                ins.then_inc(sem.handle, by)


def param_rows():
    layer = [("g_ffn1_pre", 8), ("g_ffn1_post", 8), ("g_mix_pre", 8), ("g_mla_q", 3), ("g_mla_kv", 2),
             ("w_conv", 6), ("g_mix_post", 8), ("g_ffn2_pre", 8), ("g_ffn2_post", 8), ("g_ple_pre", 8),
             ("g_ple_post", 8)]
    second = [[("g_mix_pre_2", 8), ("g_mix_post_2", 8), ("pool_scale_2", 4), ("conv_w_2", 32),
               ("conv_b_2", 8), ("b_rg_gates_2", 16), ("lru_lambda_2", 8), ("g_ffn_pre_2", 8)],
              [("g_ffn_post_2", 8), ("ffn_conv_w_2", 72), ("ffn_conv_b_2", 24), ("g_ple_gate_2", 8),
               ("g_ple_post_2", 8)]]
    return layer, second


def build_program(nc, a, consts_dram, out):
    pr = Program()
    with ExitStack() as ctx:
        def sem(name):
            return pr.sem(ctx.enter_context(nc.semaphore(name)))

        base = 16 * 1024 + 128
        KB = 1024
        cursor = [base]

        def take(size):
            at = cursor[0]
            cursor[0] += (size + 31) // 32 * 32
            assert cursor[0] <= nc.sbuf_usable_end, (cursor[0], nc.sbuf_usable_end)
            return at

        def at(name, shape, dt, offset):
            return nc.alloc_sbuf_tensor_at(name, shape, dt, offset=offset)

        def sb(name, shape, dt=F32):
            size = 4
            for s in shape[1:]:
                size *= s
            return at(name, shape, dt, take(size))

        X = sb("X", [P, DC, T])
        HH = sb("HH", [P, DC, T], F32R)
        HL = sb("HL", [P, DC, T], F32R)
        hid_at = take(96 * KB)
        raw = [sb(f"raw{i}", [P, UNIT]) for i in range(NRAW)]
        WH = [sb(f"WH{i}", [P, UNIT], F32R) for i in range(NSPLIT)]
        WL = [sb(f"WL{i}", [P, UNIT], F32R) for i in range(NSPLIT)]
        R = sb("R", [P, T])
        RP = sb("RP", [P, T])
        G = [sb(f"G{i}", [P, T]) for i in range(2)]
        U = [sb(f"U{i}", [P, T]) for i in range(2)]
        rope_at = take(4 * KB)
        consts = sb("consts", [P, CONSTS])
        par = sb("par", [P, 2 * 75 + 160 + 120])
        pcur = sb("pcur", [P, 75])
        ppost = sb("ppost", [P, DC])
        eps = sb("eps", [P, 1])
        tiny = sb("tiny", [P, 1])
        first_means = sb("first_means", [P, 16])
        stats = sb("stats", [P, 12])
        masks = sb("masks", [P, 3, P], F32R)

        ident = consts[:, 0:P]
        ones = consts[:, P:2 * P]
        nones = consts[:, 2 * P:3 * P]
        ntri = consts[:, 3 * P:4 * P]
        mask01 = consts[:, 4 * P:5 * P]
        rot = consts[:, 7 * P:8 * P]
        inv_count = consts[:, 8 * P + 1:8 * P + 17]
        inv = consts[:, 8 * P:8 * P + 1]
        identr, mask_sb, mask_mla = masks[:, 0, :], masks[:, 1, :], masks[:, 2, :]
        cosT = at("cosT", [P, T], F32, rope_at)
        sinT = at("sinT", [P, T], F32, rope_at + 2 * KB)

        HIDH = at("HIDH", [P, 24, T], F32R, hid_at)
        HIDL = at("HIDL", [P, 24, T], F32R, hid_at + 48 * KB)
        Y = at("Y", [P, DC, T], F32, hid_at)
        SQ = [G[0], G[1]]
        ACC = U[0]

        ps = [ctx.enter_context(nc.psum_tensor(f"ps{i}", [P, T], F32)) for i in range(8)]

        s_raw = [sem(f"s_raw{i}") for i in range(NRAW)]
        s_hi = sem("s_hi")
        s_lo = sem("s_lo")
        s_mm = sem("s_mm")
        s_t = sem("s_t")
        s_a = sem("s_a")
        s_d = sem("s_d")
        s_p = sem("s_p")
        s_par = sem("s_par")
        s_const = sem("s_const")
        s_x = sem("s_x")
        s_pos = sem("s_pos")
        s_ptok = sem("s_ptok")
        s_rope = sem("s_rope")
        s_out = sem("s_out")
        n_fetch = pr.sem(None)
        n_used = pr.sem(None)

        def A(build, *wait):
            return pr.put("scalar", build, wait, s_a, 1)

        def V(build, *wait):
            return pr.put("vector", build, wait, s_d, 1)

        def G_(build, *wait):
            return pr.put("gpsimd", build, wait, s_p, 1)

        def TE(build, *wait):
            return pr.put("tensor", build, wait, s_t, 1)

        def mm(build, *wait):
            pr.put("tensor", build, wait, None, 0)

        def dma(build, s, *wait):
            return pr.put("sync", build, wait, s, 16)

        pr.put("sync", lambda e, r: e.sem_inc(s_lo.handle, NRAW), (), None, 0)
        pr.put("sync", lambda e, r: e.sem_inc(s_mm.handle, SEGS * NSPLIT), (), None, 0)
        s_lo.levels[0] = NRAW
        s_mm.levels[0] = SEGS * NSPLIT

        released = []

        def fetch(parts):
            u = sum(n_fetch.levels)
            r, s = u % NRAW, u % NSPLIT
            slot_free = pr.now(s_lo).less(NRAW - 1)
            size = 0
            for src, shape in parts:
                n = 1
                for k in shape:
                    n *= k
                dst = raw[r][:, size:size + n]
                if len(shape) == 2:
                    dst = dst.rearrange("p (k n) -> p k n", k=shape[0])

                def prepare(e, reg, dst=dst, src=src):
                    weights = src(e, reg)
                    return lambda e, reg: e.dma_start(dst, weights)
                landed = dma((prepare,), s_raw[r], slot_free)
                size += n
            free = (released.pop(0) if released else
                    Mark(s_mm, [SEGS * c for c in n_fetch.levels], list(pr.loops), SEGS))
            hi = pr.put("scalar", lambda e, reg: e.activation(WH[s][:, 0:size], raw[r][:, 0:size], ACT.Copy),
                        (landed, free), s_hi, 1)
            pr.put("vector", lambda e, reg: e.tensor_tensor(WL[s][:, 0:size], raw[r][:, 0:size],
                                                            WH[s][:, 0:size].bitcast(F32), ALU.subtract),
                   (hi,), s_lo, 1)
            n_fetch.levels[-1] += 1

        def use_unit(segments, first_waits=()):
            u = sum(n_used.levels)
            s = u % NSPLIT
            split = Mark(s_lo, list(n_used.levels), list(pr.loops), NRAW + 1)
            wait0 = [split, *first_waits]
            ends = []
            assert len(segments) == SEGS
            for waits, tiles in segments:
                wait0 += waits
                for n, (o, w, ah, al, start, stop, *ready) in enumerate(tiles):
                    wait0 += ready[0] if ready else []
                    if w is None:
                        hi_, lo_ = ah
                        mh, ml = al(WH[s]), al(WL[s])
                        trio = [(hi_, mh), (lo_, mh), (hi_, ml)]
                    else:
                        wh, wl = w(WH[s]), w(WL[s])
                        trio = [(wh, ah), (wl, ah), (wh, al)]
                    for m, (lhs, rhs) in enumerate(trio):
                        last = n == len(tiles) - 1 and m == 2

                        def go(e, reg, o=o, lhs=lhs, rhs=rhs, st=start and m == 0, sp=stop and m == 2):
                            rr = rhs(reg) if callable(rhs) else rhs
                            return e.matmul(o, lhs, rr, start=st, stop=sp)
                        pr.put("tensor", go, wait0, s_mm if last else None, 1)
                        wait0 = []
                ends.append(pr.now(s_mm))
            n_used.levels[-1] += 1
            return ends

        def staged_units(stages):
            u = sum(n_used.levels)
            split = [Mark(s_lo, list(n_used.levels), list(pr.loops), NRAW + 1 + q) for q in range(NSPLIT)]
            w_, ends = [], []
            assert len(stages) == SEGS
            for stage in stages:
                freed = []
                for q, (waits, tiles) in enumerate(stage):
                    s = (u + q) % NSPLIT
                    w_ += waits + (split[q:q + 1] if stage is stages[0] else [])
                    for n, (o, w, ah, al, start, stop) in enumerate(tiles):
                        for m, (lhs, rhs) in enumerate([(w(WH[s]), ah), (w(WL[s]), ah), (w(WH[s]), al)]):
                            last = n == len(tiles) - 1 and m == 2
                            pr.put("tensor", lambda e, reg, o=o, lhs=lhs, rhs=rhs, st=start and m == 0,
                                   sp=stop and m == 2: e.matmul(o, lhs, rhs, start=st, stop=sp),
                                   w_, s_mm if last else None, 1)
                            w_ = []
                    freed.append(pr.now(s_mm))
                ends.append(freed[-1])
            released[:] = freed
            n_used.levels[-1] += NSPLIT
            return ends

        def last_units(first, nk, act, waits=None, bank_waits=None):
            stages = []
            for pair in range(DC // 2):
                stage = []
                for q in range(NSPLIT):
                    k = first + q
                    w_ = list(waits[q]) if waits and pair == 0 else []
                    w_ += bank_waits[2 * pair] + bank_waits[2 * pair + 1] if bank_waits and q == 0 else []
                    stage.append((w_, [(ps[b][:], (lambda W, b=b: W[:, b * P:(b + 1) * P]), act(k)[0], act(k)[1],
                                        k == 0, k == nk - 1) for b in (2 * pair, 2 * pair + 1)]))
                stages.append(stage)
            return staged_units(stages)

        def rows(name, first, k, col, width, layer=None, rows_per_layer=0):
            ap = a[name].rearrange("l k n -> (l k) n")

            def src(e, reg):
                f = first(reg) if callable(first) else first
                c = col(reg) if callable(col) else col
                if layer is not None:
                    f = reg(layer) * rows_per_layer + f
                f, c = [v if isinstance(v, int) else e.snap(v) for v in (f, c)]
                return ap[ds(f, k * P), ds(c, width)].rearrange("(k p) n -> p k n", p=P)
            return src

        sq_used = [None, None]
        first_sq = [None]
        sq_last = [None, None]
        acc_used = [None]

        def square_step(n, src, ready, *extra):
            b = n % 2
            q = A(lambda e, r: e.activation(SQ[b][:], src, ACT.Square), ready, sq_used[b], *extra)
            if n == 0:
                first_sq[0] = q
                return None
            if n == 1:
                p_ = G_(lambda e, r: e.tensor_tensor(ACC[:], SQ[0][:], SQ[1][:], ALU.add), first_sq[0], q,
                        acc_used[0], *extra)
                sq_used[0] = p_
            elif n < DC - 2:
                p_ = G_(lambda e, r: e.tensor_tensor(ACC[:], ACC[:], SQ[b][:], ALU.add), q, pr.now(s_p))
            else:
                sq_last[b] = q
                return pr.now(s_p)
            sq_used[b] = p_
            return p_

        def prep_chunk(n, gain, ready, free):
            h = A(lambda e, r: e.activation(HH[:, n, :], X[:, n, :], ACT.Copy, scale=gain(n)), ready, *free)
            lo = V(lambda e, r: e.scalar_tensor_tensor(out=HL[:, n, :], in0=X[:, n, :], scalar=gain(n),
                                                       in1=HH[:, n, :].bitcast(F32), op0=ALU.mult,
                                                       op1=ALU.subtract), h)
            return lo

        def ln_exp_table():
            pr.put("scalar", lambda e, r: e.preload_act_table_set("natural_log_exp_and_others"), (), None, 0)

        def done():
            return [pr.now(s_t), pr.now(s_a), pr.now(s_d), pr.now(s_p)]

        c_in = dma(lambda e, r: e.dma_start(consts[:], consts_dram), s_const)
        posi = at("posi", [P, T], I32, hid_at + 18 * KB)
        pos_in = dma(lambda e, r: e.dma_start(posi[:], a["positions"].to_broadcast([P, T])), s_pos)
        xtok = at("xtok", [P, TC, D], F32, hid_at + 32 * KB)
        x_in = [dma(lambda e, r, t=t: e.dma_start(xtok[:, t, :], a["x"][0, t * P:(t + 1) * P, :]), s_x)
                for t in range(TC)][-1]
        layer_rows, second_rows = param_rows()
        ptile = at("ptile", [P, 4, P], F32, hid_at + 16 * KB)
        cp, cs = {}, {}
        widths = [sum(k for _, k in layer_rows)] * LAYERS

        def param_dma(dst, src):
            return pr.put("scalar", lambda e, r: e.dma_start(dst, src), (), s_par, 16)

        at_row = 0
        for name, k in layer_rows:
            src = a[name] if len(a[name].shape) == 3 else a[name].rearrange("l (a n) -> l a n", a=1)
            par_in = param_dma(ptile[at_row:at_row + k, 0:LAYERS, :], src.rearrange("l a (r p) -> (a r) l p", p=P))
            cp[name] = at_row
            at_row += k
        for tno, part in enumerate(second_rows):
            at_row = 0
            for name, k in part:
                src = a[name][0]
                src = (src.rearrange("(a r p) -> (a r) p", a=1, p=P) if len(src.shape) == 1
                       else src.rearrange("a (r p) -> (a r) p", p=P))
                par_in = param_dma(ptile[at_row:at_row + k, LAYERS + tno, :], src)
                cs[name] = sum(widths) + at_row
                at_row += k
            widths.append(at_row)

        V(lambda e, r: e.memset(eps[:], EPS))
        V(lambda e, r: e.memset(tiny[:], 1e-37))
        for zero in (Y[:], ACC[:], SQ[0][:], SQ[1][:], pcur[:]):
            G_(lambda e, r, zero=zero: e.memset(zero, 0.0))
        TWO_PI = 6.283185307179586
        C1 = 6.28125
        C2 = 0.0019350051879882812
        C3 = TWO_PI - C1 - C2
        MAGIC = 1.5 * 2.0 ** 23
        rows32 = slice(HD, HD + ROPE)
        ang = at("ang", [P, T], F32, hid_at + 20 * KB)
        turns = at("turns", [P, T], F32, hid_at + 22 * KB)
        m = V(lambda e, r: e.tensor_copy(ang[:], posi[:]), pos_in)
        m = V(lambda e, r: e.tensor_scalar(ang[:], ang[:], inv, None, ALU.mult), m, c_in)
        for table, quarter in ((sinT, 0.0), (cosT, 0.25)):
            m = V(lambda e, r, q=quarter: e.tensor_scalar(turns[:], ang[:], 1.0 / TWO_PI, q,
                                                          ALU.mult, ALU.add), m)
            m = V(lambda e, r: e.tensor_scalar(turns[:], turns[:], MAGIC, MAGIC, ALU.add,
                                               ALU.subtract), m)
            m = V(lambda e, r, t=table: e.scalar_tensor_tensor(out=t[:], in0=turns[:], scalar=-C1,
                                                               in1=ang[:], op0=ALU.mult, op1=ALU.add), m)
            for c in (-C2, -C3):
                m = V(lambda e, r, t=table, c=c: e.scalar_tensor_tensor(
                    out=t[:], in0=turns[:], scalar=c, in1=t[:], op0=ALU.mult, op1=ALU.add), m)
            m = V(lambda e, r, t=table, q=quarter: e.tensor_scalar(t[:], t[:], q * TWO_PI, 3.1415925,
                                                                   ALU.add, ALU.min), m)
            m = V(lambda e, r, t=table: e.tensor_scalar(t[:], t[:], -3.1415925, None, ALU.max), m)
            A(lambda e, r, t=table: e.activation(t[:], t[:], ACT.Sin), m)

        x_done = []
        for n in range(DC):
            b = 4 + n % 4
            for t in range(TC):
                last = t == TC - 1
                (TE if last else mm)(
                    lambda e, r, n=n, t=t, b=b: e.transpose(ps[b][:, t * P:(t + 1) * P],
                                                            xtok[:, t, n * P:(n + 1) * P], ident),
                    x_in, c_in, *(x_done[n - 4:n - 3] if n >= 4 else ()))
            x_done.append(V(lambda e, r, n=n, b=b: e.tensor_copy(X[:, n, :], ps[b][:]), pr.now(s_t)))
        for i, c0 in enumerate((0, 5 * P, 6 * P)):
            A(lambda e, r, i=i, c0=c0: e.activation(masks[:, i, :], consts[:, c0:c0 + P], ACT.Copy), c_in)
        col = 0
        for tno, w in enumerate(widths):
            t = TE(lambda e, r, tno=tno, w=w: e.transpose(ps[tno][:, 0:w], ptile[0:w, tno, :], ident[0:w, 0:w]), par_in)
            V(lambda e, r, tno=tno, w=w, col=col: e.tensor_copy(par[:, col:col + w], ps[tno][:, 0:w]), t)
            col += w
        params = pr.now(s_d)
        for l in range(LAYERS):
            for name in ("g_ffn1_post", "g_ffn2_post"):
                c0 = l * widths[0] + cp[name]
                V(lambda e, r, c0=c0: e.tensor_scalar(par[:, c0:c0 + 8], par[:, c0:c0 + 8], 0.5, None, ALU.mult), params)

        def prep(gain, free, post, units, after=()):
            outs, sq = [], None
            for n0 in range(0, DC, 2):
                pair = (n0, n0 + 1)
                ready = [post(n) for n in pair]
                if n0 and units:
                    fetch(units.pop(0))
                outs += [prep_chunk(n, gain, ready[n - n0], free) for n in pair]
                for n in pair:
                    sq = square_step(n, X[:, n, :], ready[n - n0])
                if n0 // 2 < len(after):
                    after[n0 // 2]()
            while units:
                fetch(units.pop(0))
            return outs, sq

        def group_unit(kcs, wat, banks, nk, act, ready, bank_waits):
            segs = []
            for bi, bank in enumerate(banks):
                tiles = [(ps[bank][:], (lambda W, j=j, bi=bi: wat(W, j, bi)), act[0][:, kc, :], act[1][:, kc, :],
                          kc == 0, kc == nk - 1, [ready[kc]] if ready and bi == 0 else []) for j, kc in enumerate(kcs)]
                segs.append((list(bank_waits[bi] if kcs[0] == 0 else []), tiles))
            return segs

        def ev_waits():
            return [[pr.now(s_ev).less(3 - b)] for b in range(4)]

        def EV(build, *wait):
            return pr.put("vector", build, wait, s_ev, 1)

        def full_unit(kc, nk, act, waits, bank_waits, width=P, wcol=None):
            wcol = wcol or (lambda W, b: W[:, b * width:(b + 1) * width])
            segs = []
            for sgm in range(SEGS):
                tiles = []
                for b in (2 * sgm, 2 * sgm + 1):
                    tiles.append((ps[b][0:width, :], (lambda W, b=b: wcol(W, b)), act(kc)[0], act(kc)[1],
                                  kc == 0, kc == nk - 1))
                segs.append(((bank_waits[2 * sgm] + bank_waits[2 * sgm + 1] if kc == 0 else []) +
                             (waits if sgm == 0 else []), tiles))
            return segs

        HIDHf = HIDH[:, :, :].rearrange("p c t -> p (c t)")
        HIDLf = HIDL[:, :, :].rearrange("p c t -> p (c t)")

        def hid(k):
            if callable(k):
                return (lambda reg: HIDHf[:, ds(k(reg) * T, T)], lambda reg: HIDLf[:, ds(k(reg) * T, T)])
            return HIDH[:, k, :], HIDL[:, k, :]

        def down(n_hidden, n_peel, fetch_unit, early, late):
            free = ev_waits() + [[pr.now(s_ev).less(3)]] * 4

            def one(k, kk, waits, ahead):
                segs = []
                for sgm in range(SEGS):
                    tiles = [(ps[b][:], (lambda W, b=b: W[:, b * P:(b + 1) * P]), hid(kk)[0], hid(kk)[1],
                              k == 0, k == n_hidden - 1) for b in (2 * sgm, 2 * sgm + 1)]
                    segs.append(((free[2 * sgm] + free[2 * sgm + 1] if k == 0 else []) + (waits if sgm == 0 else []),
                                 tiles))
                ends = use_unit(segs)
                ahead()
                return ends

            for k in range(n_peel):
                one(k, k, early if k == 0 else [], lambda: fetch(fetch_unit(k + NSPLIT)))
            trips = (n_hidden - NSPLIT - n_peel) // NSPLIT
            assert n_peel + NSPLIT * (trips + 1) == n_hidden
            loop = pr.begin(trips)
            for m_ in range(NSPLIT):
                k0 = n_peel + m_
                one(-1, lambda reg, k0=k0: reg(loop) * NSPLIT + k0, [],
                    lambda: fetch(fetch_unit(lambda reg, k0=k0: reg(loop) * NSPLIT + (k0 + NSPLIT))))
            pr.end()
            return last_units(n_hidden - NSPLIT, n_hidden, hid, [[], [], late, []])

        def evacuate_y(ends):
            evs, sq = [], None
            ln_exp_table()
            for n in range(0, DC, 2):
                copy = lambda n, *wait: V(lambda e, r: e.tensor_copy(Y[:, n, :], ps[n][:]), ends[n // 2], *wait)
                sq = square_step(n, ps[n][:], ends[n // 2])
                squared = pr.now(s_a)
                copied = copy(n + 1)
                evs.append(copy(n, squared))
                sq = square_step(n + 1, ps[n + 1][:], copied)
                evs.append(pr.now(s_a))
            return evs, sq

        def update_x(gain, rp):
            def post(n):
                y = V(lambda e, r: e.scalar_tensor_tensor(out=Y[:, n, :], in0=Y[:, n, :], scalar=gain(n), in1=RP[:],
                                                          op0=ALU.mult, op1=ALU.mult), rp)
                return V(lambda e, r: e.tensor_tensor(X[:, n, :], X[:, n, :], Y[:, n, :], ALU.add), y)
            return post

        def rms(dst, bank, width, sq, *free):
            mm(lambda e, r: e.matmul(ps[bank][:], ones, ACC[:], start=True, stop=False), sq, *free)
            for b in range(2):
                t = TE(lambda e, r, b=b: e.matmul(ps[bank][:], ones, SQ[b][:], start=False, stop=b == 1), sq_last[b])
            acc_used[0] = sq_used[0] = sq_used[1] = t
            return rstd(dst, bank, width, t)

        def rstd(dst, bank, width, t):
            ln = A(lambda e, r: e.activation(dst[:], ps[bank][:], ACT.Ln, bias=eps[:, 0:1], scale=1.0 / width), t)
            return A(lambda e, r: e.activation(dst[:], dst[:], ACT.Exp, scale=-0.5), ln)

        def keep_warm(n, *wait):
            for _ in range(n):
                mm(lambda e, r: e.matmul(ps[3][:, 0:3 * P], identr, masks[:].rearrange("p a b -> p (a b)"), start=True,
                                         stop=True), *wait)

        def stage_end(ends, units, gain, post_gain, fill=None):
            evs, sq = evacuate_y(ends)
            todo = list(units)
            fetch(todo.pop(0))
            if fill:
                fetch(todo.pop(0))
            rp = rms(RP, 4, D, sq, evs[4])
            if fill:
                after = fill(evs, rp)
            else:
                after = ()
                keep_warm(24)
            h, sq = prep(gain, [], update_x(post_gain, rp), todo, after)
            return h, sq, evs, [evs[b:b + 1] for b in range(4)]

        def stage_start(units, gain, first):
            ln_exp_table()
            todo = list(units)
            fetch(todo.pop(0))
            sq_last[:] = [pr.now(s_a)] * 2
            rp = rms(RP, 4, D, None, *first)
            keep_warm(24)
            h, sq = prep(gain, first, update_x(lambda n: ppost[:, n:n + 1], rp), todo)
            return h, sq

        def swiglu_groups(h, sq, first_free, gate_up, n_groups, hidden_chunk, next_units, r_free):
            wat = lambda W, j, b: W[:, ds((b % 2) * 512 + j * 256 + (b // 2) * P, P)]
            marks = []

            def one(g, first, ahead):
                r_m = None
                for kp in range(4):
                    ends = use_unit(group_unit((2 * kp, 2 * kp + 1), wat, (0, 1, 2, 3), DC, (HH, HL), h if first else [],
                                               first_free if first else ev_waits()))
                    if first and kp == 2:
                        r_m = rms(R, 7, D, sq, *r_free)
                    if kp < 3:
                        ahead(kp)
                hidden_chunk(g, ends, r_m, lambda: ahead(3))
                marks.append(pr.now(s_d))

            one(0, True, lambda kp: fetch(gate_up(1)[kp]))
            loop = pr.begin(n_groups - 2)
            gi = lambda reg: reg(loop) + 1
            one(gi, False, lambda kp: fetch(gate_up(lambda reg: reg(loop) + 2)[kp]))
            pr.end()
            body = marks[-1]
            one(n_groups - 1, False, lambda kp: fetch(next_units[kp]))
            return body, marks[-1]

        def gate_up_units(gate, up, up_col, layer):
            def units(g):
                col0 = (lambda reg: g(reg) * 256) if callable(g) else g * 256
                col1 = (lambda reg: g(reg) * 256 + up_col) if callable(g) else g * 256 + up_col
                return [[(rows(gate, kp * 256, 2, col0, 256, layer, D), (2, 256)),
                         (rows(up, kp * 256, 2, col1, 256, layer, D), (2, 256))] for kp in range(4)]
            return units

        def down_unit(name, n_rows, layer):
            def unit(k):
                first = (lambda reg: k(reg) * P) if callable(k) else k * P
                return [(rows(name, first, 1, 0, D, layer, n_rows), (1, D))]
            return unit

        def hid_slot(tile, g, j):
            first = (lambda reg: (g(reg) * 2 + j) * T) if callable(g) else (lambda reg: (g * 2 + j) * T)
            return lambda reg: tile[:, ds(first(reg), T)]

        def silu_chunk(g, ends, r_m, ahead):
            s_ = []
            for j in range(2):
                gm = EV(lambda e, r, j=j: e.tensor_tensor(G[j][:], ps[2 * j][:], R[:], ALU.mult), ends[2 * j], r_m)
                um = EV(lambda e, r, j=j: e.tensor_tensor(U[j][:], ps[2 * j + 1][:], R[:], ALU.mult), ends[2 * j + 1])
                s_.append((A(lambda e, r, j=j: e.activation(G[j][:], G[j][:], ACT.Silu), gm), um))
            ahead()
            fs = [V(lambda e, r, j=j: e.tensor_tensor(U[j][:], U[j][:], G[j][:], ALU.mult), *s_[j]) for j in range(2)]
            for j in range(2):
                hh = A(lambda e, r, j=j: e.activation(hid_slot(HIDHf, g, j)(r), U[j][:], ACT.Copy), fs[j])
                V(lambda e, r, j=j: e.tensor_tensor(hid_slot(HIDLf, g, j)(r), U[j][:],
                                                    hid_slot(HIDHf, g, j)(r).bitcast(F32), ALU.subtract), hh)

        PTOK = at("PTOK", [P, TC, PLE], F32, hid_at + 44 * KB)
        PTL = at("PTL", [P, 2, T], F32R, hid_at + 44 * KB)
        PTH = at("PTH", [P, 2, T], F32R, hid_at + 92 * KB)
        E = at("E", [P, DC, T], F32, hid_at + 16 * KB)
        wat4 = lambda W, j, b: W[:, j * 512 + b * P:j * 512 + b * P + P]

        def embeddings(landed, bank, free):
            for c in range(2):
                for t in range(TC):
                    (TE if t == TC - 1 else mm)(
                        lambda e, r, c=c, t=t: e.transpose(ps[bank + c][:, t * P:(t + 1) * P],
                                                           PTOK[:, t, c * P:(c + 1) * P], ident), landed, *free)
            t_ = pr.now(s_t)
            for c in range(2):
                hh = A(lambda e, r, c=c: e.activation(PTH[:, c, :], ps[bank + c][:], ACT.Copy), t_)
                V(lambda e, r, c=c: e.tensor_tensor(PTL[:, c, :], ps[bank + c][:], PTH[:, c, :].bitcast(F32),
                                                    ALU.subtract), hh)

        def gate_group(banks, bank_waits):
            return staged_units([[(bank_waits[bi] if kp == 0 else [],
                                   [(ps[b][:], (lambda W, j=j, bi=bi: wat4(W, j, bi)), HH[:, 2 * kp + j, :],
                                     HL[:, 2 * kp + j, :], kp == j == 0, kp == 3 and j == 1) for j in range(2)])
                                  for kp in range(4)] for bi, b in enumerate(banks)])

        def ple_units(proj, gate, layer):
            col = lambda name, k, c: [(rows(name, k * P, 2, c, 512, layer, a[name].shape[1]), (2, 512))]
            return [col(proj, 0, c) for c in (0, 512)], [col(gate, 2 * kp, c) for c in (0, 512) for kp in range(4)]

        def embedding_products(free, eb):
            written = pr.now(s_d)
            ends = []
            for b0 in (0, 4):
                ends += use_unit([([*free[b0 + b], written],
                                   [(ps[b0 + b][:], (lambda W, j=j, b=b: wat4(W, j, b)), PTH[:, j, :], PTL[:, j, :],
                                     j == 0, j == 1) for j in range(2)]) for b in range(4)])

            def copies(b0):
                return lambda: eb.extend([A(lambda e, r, b=b: e.activation(E[:, b, :], ps[b][:], ACT.Copy), ends[b])
                                          for b in range(b0, b0 + 4)])
            return copies(0), copies(4)

        pcol = lambda name: (lambda n, c=cp[name]: pcur[:, c + n:c + n + 1])
        scol = lambda name: (lambda n, c=cs[name]: par[:, c + n:c + n + 1])
        s_ev = sem("s_ev")

        ready0 = done()
        layer = pr.begin(LAYERS)
        start = done()
        keep_gain = V(lambda e, r: e.tensor_copy(ppost[:], pcur[:, cp["g_ple_post"]:cp["g_ple_post"] + DC]), *ready0, *start)
        pc = V(lambda e, r: e.tensor_copy(pcur[:], par[:, ds(r(layer) * widths[0], widths[0])]), keep_gain)
        gu1 = gate_up_units("w1_gate", "w1_up", 0, layer)
        dn1 = down_unit("w1_down", FF, layer)
        h, sq = stage_start(gu1(0), pcol("g_ffn1_pre"), [*start, pc])
        early, late = swiglu_groups(h, sq, [start] * 4, gu1, FF // 256, silu_chunk, [dn1(k) for k in range(4)], start)
        win_units = [[(rows("w_in", kp * 256, 2, c, 512, layer, D), (2, 512))] for c in (512, 1024, 1440)
                     for kp in range(4)]
        win_units += [[(rows("w_in", kp * 256, 2, 1952, 256, layer, D), (2, 256))] for kp in range(4)]
        win_units += [[(rows("w_in", kp * 256, 2, 0, 512, layer, D), (2, 512))] for kp in range(4)]
        ends = down(FF // P, 2, dn1, [early], [late])
        h, sq, evs, free = stage_end(ends, win_units[0:4], pcol("g_mix_pre"), pcol("g_ffn1_post"))

        def mixer_tile(name, shape, kb, dt=F32):
            return at(name, shape, dt, hid_at + int(kb * KB))

        QS = mixer_tile("QS", [P, 2, T], 0)
        KS = mixer_tile("KS", [P, 2, T], 4)
        VS = mixer_tile("VS", [P, TC, 256], 8)
        QM = mixer_tile("QM", [P, MLA_HEADS, T], 12)
        KM = mixer_tile("KM", [P, MLA_HEADS, T], 28)
        VF = mixer_tile("VF", [P, 2, T], 28)
        VM = mixer_tile("VM", [P, TC, 512], 44)
        KR = mixer_tile("KR", [P, T], 52)
        CQ = mixer_tile("CQ", [P, 5, T], 54)
        CH = mixer_tile("CH", [P, 5, T], 64, F32R)
        CL = mixer_tile("CL", [P, 5, T], 74, F32R)
        CS = mixer_tile("CS", [P, 5, T], 64)
        CV = mixer_tile("CV", [P, 6, T], 84)
        QR = mixer_tile("QR", [P, 2, T], 84)
        PB = [mixer_tile(f"PB{i}", [P, T], 54 + 2 * i) for i in range(4)]
        PT = [mixer_tile(f"PT{i}", [P, TC, T], 62 + 8 * i) for i in range(2)]
        SP = [mixer_tile(f"SP{i}", [P, T], 78 + 2 * i) for i in range(2)]
        SS = [mixer_tile(f"SS{i}", [P, T], 82 + 2 * i) for i in range(2)]
        SW = mixer_tile("SW", [P, TC, T], 86)

        wat = lambda W, j, b: W[:, j * 512 + b * P:j * 512 + b * P + P]

        def win_group(no, keep, w=wat, banks=(0, 1, 2, 3), hook=None, bank_waits=None):
            r_m = None
            for kp in range(4):
                segs = group_unit((2 * kp, 2 * kp + 1), w, banks, DC, (HH, HL), h if no == 0 else [],
                                  free if no == 0 else bank_waits or ev_waits())
                while len(segs) < SEGS:
                    segs = [(w_ if not i_ else [], [t]) for w_, ts in segs for i_, t in enumerate(ts)]
                e_ = use_unit(segs)
                if no == 0 and kp == 2:
                    r_m = rms(R, 7, D, sq, evs[7])
                if kp in (hook or {}):
                    hook[kp]()
                if kp < 3:
                    fetch(ahead_units[4 * no + kp])
            kept = keep(e_, r_m)
            fetch(ahead_units[4 * no + 3])
            return kept

        def take_r(dst, bank, end, *wait):
            return EV(lambda e, r: e.tensor_tensor(dst, ps[bank][:], R[:], ALU.mult), end, *wait)

        def head_cols(name, per_layer, k, width, lo, hi):
            ap = a[name].rearrange("l k (h c) -> (l k) h c", c=width)
            return (lambda e, reg: ap[ds(e.snap(reg(layer) * per_layer + k * P), P), :, lo:hi]), (MLA_HEADS, hi - lo)
        lat_units = [[head_cols("w_mla_uq", Q_RANK, k, QK, HD, QK) for k in range(3)]]
        lat_units += [[head_cols("w_mla_uq", Q_RANK, k, QK, 0, HD)] for k in range(3)]
        lat_units += [[head_cols("w_mla_ukv", PLE, k, 2 * HD, lo, lo + HD) for k in range(2)] for lo in (0, HD)]
        out_units = [[(rows("w_out", k * P, 1, 0, D, layer, D), (1, D))] for k in range(8)]
        ahead_units = win_units[4:] + lat_units[0:4]

        def keep(ends, r_m):
            return [take_r(VF[:, j, :], j, ends[j], r_m) for j in range(2)] + [
                take_r(CQ[:, j, :], 2 + j, ends[2 + j]) for j in range(2)] + [r_m]
        _, vf1, cq0, cq1, r_m = win_group(0, keep)

        wr = lambda W, j, b: W[:, j * 512 + (b * P if b < 3 else 320):j * 512 + (b * P if b < 3 else 320) + P]

        def keep(ends, _):
            cq = [cq0, cq1] + [take_r(CQ[:, 2 + j, :], j, ends[j]) for j in range(3)]
            kr = EV(lambda e, r: e.tensor_tensor(KR[rows32, :], ps[3][rows32, :], R[rows32, :], ALU.mult), ends[3])
            q_ = [A(lambda e, r, c=c: e.activation(CS[:, c, :], CQ[:, c, :], ACT.Square), cq[c]) for c in range(5)]
            p_ = G_(lambda e, r: e.tensor_tensor(CS[:, 0, :], CS[:, 0, :], CS[:, 1, :], ALU.add), q_[0], q_[1])
            p_ = G_(lambda e, r: e.tensor_tensor(CS[:, 0, :], CS[:, 0, :], CS[:, 2, :], ALU.add), q_[2], p_)
            return kr, p_, G_(lambda e, r: e.tensor_tensor(CS[:, 3, :], CS[:, 3, :], CS[:, 4, :], ALU.add), q_[3], q_[4])
        kr, sum_q, sum_kv = win_group(1, keep, wr)

        turned_v, latent_r = [], []

        def hook():
            for j in range(2):
                for t in range(TC):
                    (TE if t == TC - 1 else mm)(
                        lambda e, r, j=j, t=t: e.transpose(ps[4 + j][:, t * P:(t + 1) * P],
                                                           VF[:, j, t * P:(t + 1) * P], ident), vf1)
                turned_v.append(V(lambda e, r, j=j: e.tensor_copy(
                    VS[:, :, j * P:(j + 1) * P], ps[4 + j][:].rearrange("p (t c) -> p t c", t=TC)), pr.now(s_t)))
            turned_v.append(TE(lambda e, r: e.matmul(ps[6][HD:P, :], rot[rows32, HD:P], KR[rows32, :], start=True,
                                                     stop=True), kr))
            for dst, bank, c, width, ready in ((RP, 7, 0, Q_RANK, (sum_q, r_m)), (U[1], 4, 3, PLE, (sum_kv, turned_v[0]))):
                t_ = TE(lambda e, r, bank=bank, c=c: e.matmul(ps[bank][:], ones, CS[:, c, :], start=True, stop=True), *ready)
                latent_r.append(rstd(dst, bank, width, t_))

        def keep(ends, _):
            return [take_r(CV[:, j, :], j, ends[j]) for j in range(4)]
        cv = win_group(2, keep, hook={1: hook})
        normed = []
        for c in range(5):
            gain, q = (pcol("g_mla_q")(c), RP) if c < 3 else (pcol("g_mla_kv")(c - 3), U[1])
            normed.append(V(lambda e, r, c=c, gain=gain, q=q: e.scalar_tensor_tensor(
                out=CQ[:, c, :], in0=CQ[:, c, :], scalar=gain, in1=q[:], op0=ALU.mult, op1=ALU.mult), latent_r[c // 3]))
        vs, krot = turned_v[1], turned_v[2]

        wh_ = lambda W, j, b: W[:, j * 256 + b * P:j * 256 + b * P + P]
        latent_in = []

        def split_latents():
            for c in range(5):
                hh = A(lambda e, r, c=c: e.activation(CH[:, c, :], CQ[:, c, :], ACT.Copy), normed[c], pr.now(s_t))
                latent_in.append(V(lambda e, r, c=c: e.tensor_tensor(CL[:, c, :], CQ[:, c, :], CH[:, c, :].bitcast(F32),
                                                                     ALU.subtract), hh))
            m1 = V(lambda e, r: e.tensor_tensor(G[0][rows32, :], ps[6][rows32, :], sinT[rows32, :], ALU.mult), krot)
            m2 = V(lambda e, r: e.tensor_tensor(KR[rows32, :], KR[rows32, :], cosT[rows32, :], ALU.mult), krot)
            m2 = V(lambda e, r: e.tensor_tensor(KR[rows32, :], KR[rows32, :], G[0][rows32, :], ALU.add), m1, m2)
            latent_in.append(m2)

        def keep(ends, _):
            return [take_r(CV[:, 4 + j, :], j, ends[2 * j + 1]) for j in range(2)]
        cv += win_group(3, keep, wh_, banks=(0, 1))

        wc = lambda k, j: pcur[:, cp["w_conv"] + 2 * k + j:cp["w_conv"] + 2 * k + j + 1]
        conv = []

        def hook():
            for j in range(2):
                u_ = V(lambda e, r, j=j: e.tensor_tensor(CV[:, 2 + j, :], CV[:, 2 + j, :], CV[:, 4 + j, :], ALU.mult),
                       cv[4 + j])
                y_ = V(lambda e, r, j=j: e.tensor_scalar(CV[:, 4 + j, :], CV[:, 2 + j, :], wc(2, j), None, ALU.mult), u_)
                for k, sh in ((1, 1), (0, 2)):
                    y_ = V(lambda e, r, j=j, k=k, sh=sh: e.scalar_tensor_tensor(
                        out=CV[:, 4 + j, sh:T], in0=CV[:, 2 + j, 0:T - sh], scalar=wc(k, j), in1=CV[:, 4 + j, sh:T],
                        op0=ALU.mult, op1=ALU.add), y_)
                conv.append(V(lambda e, r, j=j: e.tensor_tensor(CV[:, 4 + j, :], CV[:, 4 + j, :], CV[:, j, :],
                                                                ALU.mult), y_))

        def keep(ends, _):
            return [EV(lambda e, r, j=j: e.scalar_tensor_tensor(
                out=QS[:, j, :], in0=ps[j][:], scalar=HD ** -0.5, in1=R[:], op0=ALU.mult, op1=ALU.mult), ends[j])
                for j in range(2)] + [take_r(KS[:, j, :], 2 + j, ends[2 + j]) for j in range(2)]
        qk = win_group(4, keep, hook={0: hook, 2: split_latents}, bank_waits=[cv[4:5], cv[5:6], cv[2:3], cv[3:4]])
        ks = qk[2:]
        win_done = pr.now(s_mm)
        kr = latent_in[5]
        dma(lambda e, r: e.dma_start(KM[rows32, :, :], KR[rows32, :].unsqueeze(1)
                                     .to_broadcast([ROPE, MLA_HEADS, T])), s_rope, kr, vs)
        for j in range(2):
            hh = A(lambda e, r, j=j: e.activation(HH[:, 6 + j, :], CV[:, 4 + j, :], ACT.Copy), conv[j], win_done)
            conv_done = V(lambda e, r, j=j: e.tensor_tensor(HL[:, 6 + j, :], CV[:, 4 + j, :],
                                                            HH[:, 6 + j, :].bitcast(F32), ALU.subtract), hh)

        segs = [([latent_in[2]] if a_ == 0 and q == 0 else [],
                 [(ps[4 + a_][:], (lambda W, k=k, a_=a_: W[:, k * 256 + a_ * P:k * 256 + a_ * P + P]), CH[:, k, :],
                   CL[:, k, :], k == 0, k == 2) for k in ks_]) for a_ in range(2) for q, ks_ in ((0, (0, 1)), (1, (2,)))]
        ends = use_unit(segs)
        fetch(lat_units[4])
        qr = [A(lambda e, r, a_=a_: e.activation(QR[:, a_, :], ps[4 + a_][:], ACT.Copy, scale=QK ** -0.5),
                ends[2 * a_ + 1], conv_done) for a_ in range(2)]
        for k in range(3):
            ends = use_unit([([qk[b]] if k == 0 else [],
                              [(ps[b][:], (lambda W, b=b: W[:, b * P:(b + 1) * P]), CH[:, k, :], CL[:, k, :],
                                k == 0, k == 2)]) for b in range(4)])
            if k == 0:
                fetch(lat_units[5])
                qrot = [TE(lambda e, r, a_=a_: e.matmul(ps[6 + a_][:], rot, QR[:, a_, :], start=True, stop=True),
                           qr[a_], kr) for a_ in range(2)]
        qr_done = []
        rotated = [V(lambda e, r, a_=a_: e.tensor_tensor(G[a_][:], ps[6 + a_][:], sinT[:], ALU.mult), qrot[a_], kr)
                   for a_ in range(2)]
        for a_ in range(2):
            m2 = V(lambda e, r, a_=a_: e.tensor_tensor(QR[:, a_, :], QR[:, a_, :], cosT[:], ALU.mult), qrot[a_])
            m2 = V(lambda e, r, a_=a_: e.tensor_tensor(QR[:, a_, :], QR[:, a_, :], G[a_][:], ALU.add), rotated[a_], m2)
            qr_done.append(m2)

        def two_heads(dst, bank, pair, end, engine, scale):
            out_ = []
            for q in range(2):
                o, i_ = dst[0:HD, 2 * pair + q, :], ps[bank][q * HD:(q + 1) * HD, :]
                if engine is A:
                    out_.append(A(lambda e, r, o=o, i_=i_: e.activation(o, i_, ACT.Copy, scale=scale), end, vs))
                else:
                    out_.append(V(lambda e, r, o=o, i_=i_: e.tensor_scalar(o, i_, scale, None, ALU.mult), end, vs))
            return out_
        qm = [two_heads(QM, b, b, ends[b], A if b < 2 else V, QK ** -0.5) for b in range(4)]
        for hd in range(MLA_HEADS):
            q_, r_ = hd // 4, slice(hd % 4 * ROPE, (hd % 4 + 1) * ROPE)
            dma(lambda e, r, hd=hd, q_=q_, r_=r_: e.dma_start(QM[rows32, hd, :], QR[r_, q_, :]), s_rope, qr_done[q_])
        rope_in = pr.now(s_rope)
        key_free = [qr[0], qr[1], rotated[0], rotated[1]]
        key_cols = lambda k, b: (lambda W: W[:, k * 512 + b * P:k * 512 + b * P + P])
        ends = use_unit([([key_free[b], latent_in[4], qrot[1]],
                          [(ps[4 + b][:], key_cols(k, b), CH[:, 3 + k, :], CL[:, 3 + k, :], k == 0, k == 1)
                           for k in range(2)]) for b in range(4)])
        km = [two_heads(KM, 4 + b, b, ends[b], V if b < 2 else A, 1.0) for b in range(4)]
        segs = []
        for t in range(TC):
            sl = slice(t * P, (t + 1) * P)
            segs.append(([qm[t][1]],
                         [(ps[t][:], None, (CH[:, 3 + k, sl], CL[:, 3 + k, sl]),
                           (lambda W, k=k: W[:, k * 512:(k + 1) * 512]), k == 0, k == 1) for k in range(2)]))
        ends = use_unit(segs)
        vm = [A(lambda e, r, t=t: e.activation(VM[:, t, :], ps[t][:], ACT.Copy), ends[t]) for t in range(TC)]
        lat_in = [rope_in, *qm[1], *qm[3], *km[1], *km[3]]
        sc_read, tp_read, pb_read = vm[0:2], vm[2:4], [None] * 4
        pt_read, pv_read = [None] * 2, [km[2][1], km[3][1]]
        scored, soft, turned = {}, {}, {}
        chunk_done = {6: conv_done, 7: conv_done}

        def lat_score(n):
            hd, i, b = n // TC, n % TC, n % 2
            w_ = (i + 1) * P
            mm(lambda e, r: e.matmul(ps[b][:, 0:w_], QM[0:QK, hd, i * P:w_], KM[0:QK, hd, 0:w_],
                                     start=True, stop=False), *(lat_in if n < 2 else []), sc_read[b])
            scored[n] = TE(lambda e, r: e.matmul(ps[b][:, i * P:w_], identr, mask_mla, start=False, stop=True))

        def lat_max(n):
            b, c, w_ = n % 2, n % 4, (n % TC + 1) * P
            return V(lambda e, r: e.tensor_reduce(out=stats[:, c:c + 1], in_=ps[b][:, 0:w_], axis=AXX, op=ALU.max,
                                                  negate=True), scored[n], pb_read[c])

        def lat_exp(n, m_):
            b, c, w_ = n % 2, n % 4, (n % TC + 1) * P
            sc_read[b] = A(lambda e, r: e.activation(PB[c][:, 0:w_], ps[b][:, 0:w_], ACT.Exp, bias=stats[:, c:c + 1],
                                                     accum_out=stats[:, 4 + c:5 + c]), m_, pb_read[c])

        def lat_divide(n):
            b, c, w_ = n % 2, n % 4, (n % TC + 1) * P
            d_ = V(lambda e, r: e.reciprocal(stats[:, 8 + c:9 + c], stats[:, 4 + c:5 + c]), sc_read[b])
            soft[n] = V(lambda e, r: e.tensor_scalar(PB[c][:, 0:w_], PB[c][:, 0:w_], stats[:, 8 + c:9 + c], None,
                                                     ALU.mult), d_)

        def lat_turn(n):
            i, b, c = n % TC, 2 + n % 2, n % 4
            for j in range(i + 1):
                (TE if j == i else mm)(lambda e, r, j=j: e.transpose(
                    ps[b][:, j * P:(j + 1) * P], PB[c][:, j * P:(j + 1) * P], ident), soft[n], tp_read[b - 2])
            turned[n] = pb_read[c] = pr.now(s_t)

        def lat_keep(n):
            hd, i, b = n // TC, n % TC, 2 + n % 2
            tp_read[b - 2] = V(lambda e, r: e.tensor_copy(
                PT[hd % 2][:, 0:i + 1, i * P:(i + 1) * P],
                ps[b][:, 0:(i + 1) * P].rearrange("p (j c) -> p j c", j=i + 1)), turned[n], pt_read[hd % 2])

        def values(hd, bank, vals, weights, ready):
            rr = slice((hd % 2) * HD, (hd % 2) * HD + HD)
            for j in range(TC):
                (TE if j == TC - 1 else mm)(lambda e, r, j=j: e.matmul(
                    ps[bank][rr, j * P:T], vals[:, j, hd * HD:(hd + 1) * HD], weights[:, j, j * P:T],
                    start=j == 0, stop=j == TC - 1), *(ready if j == 0 else []), pv_read[bank - 6])
            return pr.now(s_t)

        def values_keep(hd, bank, t_, chunk):
            rr = slice((hd % 2) * HD, (hd % 2) * HD + HD)
            hh = A(lambda e, r: e.activation(HH[rr, chunk, :], ps[bank][rr, :], ACT.Copy), t_, win_done)
            chunk_done[chunk] = pv_read[bank - 6] = V(lambda e, r: e.tensor_tensor(
                HL[rr, chunk, :], ps[bank][rr, :], HH[rr, chunk, :].bitcast(F32), ALU.subtract), hh)

        T1 = (G[0], G[1])
        t1_free = [pr.now(s_d)] * 2
        z_done, sp_done, w_sum, w_done = {}, {}, {}, {-1: km[1][1]}
        sw_read, z_read, sums = [None], [None], {-1: None}

        def sb_z(m, bank, *wait):
            hd, j = m // TC, TC - 1 - m % TC
            rr = slice((hd % 2) * HD, (hd % 2) * HD + HD)
            z_done[m] = TE(lambda e, r: e.matmul(ps[bank][:, j * P:T], KS[rr, hd // 2, j * P:(j + 1) * P],
                                                 QS[rr, hd // 2, j * P:T], start=True, stop=bank == 4), *wait)

        def sb_softplus(m):
            j, b = TC - 1 - m % TC, m % 2
            z, t1 = ps[4][:, j * P:T], T1[b][:, j * P:T]
            x_ = A(lambda e, r: e.activation(t1, z, ACT.Abs), z_done[m], t1_free[b])
            x_ = A(lambda e, r: e.activation(t1, t1, ACT.Exp, scale=-1.0), x_)
            return A(lambda e, r: e.activation(t1, t1, ACT.Ln, bias=1.0), x_)

        def sb_mask(m, x_):
            j, b = TC - 1 - m % TC, m % 2
            z, t1, sp = ps[4][:, j * P:T], T1[b][:, j * P:T], SP[b]
            diag, rest = slice(j * P, (j + 1) * P), slice((j + 1) * P, T)
            d_ = V(lambda e, r: e.scalar_tensor_tensor(out=sp[:, j * P:T], in0=z, scalar=0.0, in1=t1, op0=ALU.max,
                                                       op1=ALU.add), x_, w_sum.get(m - 2), sums.get(m - 2))
            t1_free[b] = z_read[0] = d_
            sp_done[m] = V(lambda e, r: e.tensor_tensor(sp[:, diag], sp[:, diag], mask01, ALU.mult), d_)
            if j > 0:
                V(lambda e, r: e.tensor_copy(SS[b][:, diag], sp[:, diag]), sp_done[m], w_sum.get(m - 1),
                  sums.get(m - 1))
                sums[m] = pr.now(s_d)
                if j < TC - 1:
                    sums[m] = G_(lambda e, r: e.tensor_tensor(SS[b][:, rest], SS[1 - b][:, rest], sp[:, rest], ALU.add),
                                 sums[m - 1], pr.now(s_d), w_sum.get(m - 1))
            else:
                sums[m] = None

        def sb_sum(m):
            j, b = TC - 1 - m % TC, m % 2
            o = ps[5]
            sb_z(m, 5, w_done.get(m - 1))
            mm(lambda e, r: e.matmul(o[:, j * P:T], ntri, SP[b][:, j * P:T], start=False, stop=False), sp_done[m])
            if j < TC - 1:
                mm(lambda e, r: e.matmul(o[:, (j + 1) * P:T], nones, SS[1 - b][:, (j + 1) * P:T], start=False,
                                         stop=False), sums[m - 1], sp_done[m - 1])
            w_sum[m] = TE(lambda e, r: e.matmul(o[:, j * P:(j + 1) * P], identr, mask_sb, start=False, stop=True))

        def sb_exp(m):
            j, b = TC - 1 - m % TC, m % 2
            w_done[m] = A(lambda e, r: e.activation(SW[:, j, j * P:T], ps[5][:, j * P:T], ACT.Exp), w_sum[m],
                          sw_read[0])

        ROUNDS = SB_HEADS * TC
        lat_score(0)
        lat_score(1)
        sb_z(0, 4, km[0][1], ks[1])
        for rnd in range(ROUNDS + 2):
            if rnd in (1, 4, 7, 10):
                fetch(out_units[rnd // 3])
            lag = 0 < rnd <= ROUNDS
            kept = []
            if lag:
                sb_sum(rnd - 1)
                lat_turn(2 * rnd - 2)
                lat_turn(2 * rnd - 1)
            if rnd >= 3 and rnd % 2 == 1:
                hd = (rnd - 3) // 2
                pt_read[hd % 2] = values(hd, 6, VM, PT[hd % 2], [*tp_keep, vm[-1]])
                kept.append((hd, 6, pt_read[hd % 2], 2 + hd // 2))
            if rnd >= 5 and rnd % 4 == 1:
                hd = (rnd - 5) // 4
                sw_read[0] = values(hd, 7, VS, SW, [w_done[4 * hd + 3]])
                kept.append((hd, 7, sw_read[0], hd // 2))
            if rnd < ROUNDS:
                maxes = [lat_max(2 * rnd), lat_max(2 * rnd + 1)]
                lat_exp(2 * rnd, maxes[0])
                x_ = sb_softplus(rnd)
                lat_exp(2 * rnd + 1, maxes[1])
                lat_divide(2 * rnd)
                sb_mask(rnd, x_)
                lat_divide(2 * rnd + 1)
            if lag:
                sb_exp(rnd - 1)
                lat_keep(2 * rnd - 2)
                lat_keep(2 * rnd - 1)
                tp_keep = list(tp_read)
            for args in kept:
                values_keep(*args)
            if rnd < ROUNDS - 1:
                lat_score(2 * rnd + 2)
                lat_score(2 * rnd + 3)
                sb_z(rnd + 1, 4, z_read[0])

        gu2 = gate_up_units("w2_gate", "w2_up", 0, layer)
        dn2 = down_unit("w2_down", FF, layer)
        bank_w = [[w_done[14], w_done[15], tp_read[0], tp_read[1], sc_read[0], sc_read[1]]] + [[]] * 5 + [pv_read] * 2
        for k in range(4):
            use_unit(full_unit(k, 8, lambda kc: (HH[:, kc, :], HL[:, kc, :]), [chunk_done[k]], bank_w))
            fetch(out_units[4 + k])
        ends = last_units(4, 8, lambda kc: (HH[:, kc, :], HL[:, kc, :]), [[chunk_done[k]] for k in range(4, 8)])
        def load_tokens(e, reg):
            tokens = a["p"].rearrange("l b (t q) c -> (l b) q t c", q=P)[ds(e.snap(reg(layer) * 1), 1), :, :, :]
            return lambda e, reg: e.dma_start(PTOK[:], tokens.rearrange("l q t c -> (l q) t c"))
        p_in = dma((load_tokens,), s_ptok, pv_read[0], pv_read[1])
        h, sq, evs, free = stage_end(ends, gu2(0), pcol("g_ffn2_pre"), pcol("g_mix_post"))
        embeddings(p_in, 5, evs[5:8])
        early, late = swiglu_groups(h, sq, free, gu2, FF // 256, silu_chunk,
                                    [dn2(k) for k in range(4)], [evs[7]])
        pproj, gates = ple_units("w_ple_proj", "w_ple_gate", layer)
        ple_u = pproj + gates
        ends = down(FF // P, 2, dn2, [early], [late])
        eb = []
        h, sq, evs, free = stage_end(ends, ple_u[0:6], pcol("g_ple_pre"), pcol("g_ffn2_post"),
                                     fill=lambda evs, rp: embedding_products([[m_, rp] for m_ in evs], eb))
        for kp in range(4):
            e_ = use_unit(group_unit((2 * kp, 2 * kp + 1), wat4, range(4), DC, (HH, HL), h, [[m_] for m_ in eb[0:4]]))
            if kp == 2:
                r_m = rms(R, 7, D, sq, eb[7])
            if kp < 3:
                fetch(ple_u[kp + 6])
        products = []

        def scaled(n, end):
            z_ = V(lambda e, r, n=n: e.tensor_tensor(Y[:, n, :], ps[n][:], R[:], ALU.mult), end, r_m)
            products.append(A(lambda e, r, n=n: e.activation(Y[:, n, :], Y[:, n, :], ACT.Sigmoid), z_))

        def gated(n):
            z_ = V(lambda e, r, n=n: e.tensor_tensor(Y[:, n, :], Y[:, n, :], E[:, n, :], ALU.mult), products[n])
            return square_step(n, Y[:, n, :], z_)
        for n in range(4):
            scaled(n, e_[n])
        fetch(ple_u[9])
        for n in range(4):
            gated(n)
        e_ = gate_group(range(4, 8), [[eb[b], r_m] for b in range(4, 8)])
        keep_warm(16, products[3])
        for n in range(4, 8):
            scaled(n, e_[n - 4])
            gated(n)
        pr.end()
        start = done()
        LX = at("LX", [P, DC, T], F32, hid_at)
        LXH = at("LXH", [P, DC, T], F32R, hid_at)
        XC = at("XC", [P, DC, T], F32, hid_at + 16 * KB)
        UP = at("UP", [P, TC, T], F32, hid_at + 32 * KB)
        UPL = at("UPL", [P, TC, T], F32R, hid_at + 32 * KB)
        LG = at("LG", [P, DC, T], F32, hid_at + 40 * KB)
        LGL = at("LGL", [P, DC, T], F32R, hid_at + 40 * KB)
        GP = at("GP", [P, DC, T], F32, hid_at + 56 * KB)
        TH = at("TH", [P, DC, T], F32, hid_at + 72 * KB)
        GR = at("GR", [P, DC, T], F32, hid_at + 72 * KB)
        PH = at("PH", [P, TC, T], F32R, hid_at + 88 * KB)
        bd = at("bd", [P, 16, P], F32, hid_at + 88 * KB)
        pw = at("pw", [P, TC, P], F32, rope_at)
        lam = at("lam", [P, 3, 8], F32, rope_at + 2 * KB)

        win2 = lambda c: [[(rows("w_in_2", kp * 256, 2, c, 512), (2, 512))] for kp in range(4)]
        w2 = [u for c in (512, 1024, 0, 1536, 2048, 2560, 3072, 3584, 4096) for u in win2(c)]
        w2 += [[(rows("w_pool_out_2", k * P, 1, 0, D), (1, D))] for k in range(4)]
        w2 += [[(rows(w, k * P, 1, 0, D), (1, D))] for w in ("w_rg_out_2", "w_o_2") for k in range(8)]
        gu = gate_up_units("w_up_2", "w_up_2", FF2, None)
        at_unit = [0]

        def ahead():
            fetch(w2[at_unit[0]])
            at_unit[0] += 1

        bd0 = G_(lambda e, r: e.memset(bd[:], 0.0), *start)
        keep_gain = V(lambda e, r: e.tensor_copy(ppost[:], pcur[:, cp["g_ple_post"]:cp["g_ple_post"] + DC]), *start)
        h, sq = stage_start(w2[0:4], scol("g_mix_pre_2"), [*start, keep_gain])
        at_unit[0] = 4
        pw_in = dma(lambda e, r: e.dma_start(pw[:], a["pool_w_2"][0].rearrange("g c d -> c g d")), s_par, *start)
        heads = a["w_rg_gates_2"].rearrange("l g (h q) i j -> q i (l g h) j", q=2)
        bd_in = [dma(lambda e, r, q=q: e.dma_start(bd[q * HD:(q + 1) * HD, :, q * HD:(q + 1) * HD], heads[q]), s_par, bd0)
                 for q in range(2)][-1]
        lm = par[:, cs["lru_lambda_2"]:cs["lru_lambda_2"] + 8]
        l_ = A(lambda e, r: e.activation(lam[:, 2, :], lm, ACT.Abs), *start)
        l_ = A(lambda e, r: e.activation(lam[:, 2, :], lam[:, 2, :], ACT.Exp, scale=-1.0), l_)
        l_ = A(lambda e, r: e.activation(lam[:, 2, :], lam[:, 2, :], ACT.Ln, bias=1.0), l_)
        m_ = V(lambda e, r: e.tensor_scalar(lam[:, 0, :], lm, -1.0, 0.0, ALU.mult, ALU.max), *start)
        m_ = V(lambda e, r: e.tensor_tensor(lam[:, 0, :], lam[:, 0, :], lam[:, 2, :], ALU.add), l_, m_)
        l_ = V(lambda e, r: e.tensor_scalar(lam[:, 1, :], lam[:, 0, :], -LRU_C, None, ALU.mult), m_)
        lam_done = V(lambda e, r: e.tensor_scalar(lam[:, 0, :], lam[:, 0, :], LRU_C, None, ALU.mult), l_)

        def in_group(no, keep, hook=None):
            r_m = None
            for kp in range(4):
                ends = use_unit(group_unit((2 * kp, 2 * kp + 1), wat4, (0, 1, 2, 3), DC, (HH, HL),
                                           h if no == 0 else [], [start] * 4 if no == 0 else ev_waits()))
                if no == 0 and kp == 2:
                    r_m = rms(R, 7, D, sq, *start)
                if kp == 1 and hook:
                    hook()
                if kp < 3:
                    ahead()
            kept = keep(ends, r_m)
            ahead()
            return kept

        def take4(dst, c0, *waits):
            return lambda ends, r_m=None: [EV(lambda e, r, j=j: e.tensor_tensor(dst[:, c0 + j, :], ps[j][:], R[:],
                                                                                ALU.mult), ends[j], r_m, *waits)
                                           for j in range(4)]

        xc = []

        def conv4(n):
            cw = lambda k: par[:, cs["conv_w_2"] + 8 * k + n:cs["conv_w_2"] + 8 * k + n + 1]
            y_ = V(lambda e, r: e.tensor_scalar(XC[:, n, :], LX[:, n, :], cw(3), scol("conv_b_2")(n), ALU.mult,
                                                ALU.add), lx[n])
            for k, sh in ((2, 1), (1, 2), (0, 3)):
                y_ = V(lambda e, r, k=k, sh=sh: e.scalar_tensor_tensor(
                    out=XC[:, n, sh:T], in0=LX[:, n, 0:T - sh], scalar=cw(k), in1=XC[:, n, sh:T],
                    op0=ALU.mult, op1=ALU.add), y_)
            xc.append(y_)

        gate_read = {}
        scan_in, tanh_done, r_done = [], [], []
        tmp_read = [pr.now(s_p)] * 2

        def lru_gates(n):
            br, bi = 4 + 2 * (n % 2), 5 + 2 * (n % 2)
            tr = TE(lambda e, r: e.matmul(ps[br][:], bd[:, n, :], XC[:, n, :], start=True, stop=True),
                    xc[n], bd_in, r_sum, *gate_read.get(br, []))
            ti = TE(lambda e, r: e.matmul(ps[bi][:], bd[:, 8 + n, :], XC[:, n, :], start=True, stop=True),
                    *gate_read.get(bi, []))
            rg = A(lambda e, r: e.activation(LX[:, n, :], ps[br][:], ACT.Sigmoid, bias=scol("b_rg_gates_2")(n)), tr)
            ig = A(lambda e, r: e.activation(G[n % 2][:], ps[bi][:], ACT.Sigmoid, bias=scol("b_rg_gates_2")(8 + n)),
                   ti, tmp_read[n % 2])
            gate_read[br], gate_read[bi] = [rg], [ig]
            r_done.append(rg)
            tanh_done.append(A(lambda e, r: e.activation(TH[:, n, :], LX[:, n, :], ACT.Tanh,
                                                         scale=lam[:, 0, n:n + 1]), rg, lam_done))
            s_ = V(lambda e, r: e.tensor_tensor(XC[:, n, :], XC[:, n, :], G[n % 2][:], ALU.mult), ig)
            tmp_read[n % 2] = s_
            scan_in.append(s_)

        pool_d = []

        def pool(g):
            width = POOL_WINDOWS[g]
            src, m_ = UP[:, g, :], up[g]
            step, side = 1, 0
            while step < width:
                dst = (U[0], U[1])[side]
                m1 = G_(lambda e, r, d=dst, s_=src, k=step: e.tensor_tensor(d[:, k:T], s_[:, k:T], s_[:, 0:T - k],
                                                                           ALU.add), m_, *pool_d[-1:])
                m_ = G_(lambda e, r, d=dst, s_=src, k=step: e.tensor_copy(d[:, 0:k], s_[:, 0:k]), m1)
                src, step, side = dst, 2 * step, 1 - side

            def rest():
                m1 = V(lambda e, r: e.tensor_tensor(first_means[:, 0:width], src[:, 0:width], inv_count[:, 0:width],
                                                    ALU.mult), m_, *pool_d[-1:])
                m1 = V(lambda e, r: e.scalar_tensor_tensor(out=UP[:, g, width:T], in0=src[:, width:T],
                                                           scalar=1.0 / width, in1=UP[:, g, width:T], op0=ALU.mult,
                                                           op1=ALU.subtract), m1)
                pool_d.append(V(lambda e, r: e.tensor_tensor(UP[:, g, 0:width], first_means[:, 0:width],
                                                             UP[:, g, 0:width], ALU.subtract), m1))
            return rest

        def lru_pair(n):
            lru_gates(n)
            lru_gates(n + 1)

        def scan_pair(n0):
            pair = (n0, n0 + 1)
            a_, l2, d_, m_ = {}, {}, {}, {}
            for n in pair:
                b = n % 2
                a_[n] = A(lambda e, r, n=n: e.activation(LX[:, n, :], LX[:, n, :], ACT.Exp, scale=lam[:, 1, n:n + 1]),
                          tanh_done[n])
                l1 = A(lambda e, r, n=n, b=b: e.activation(G[b][:], TH[:, n, :], ACT.Ln, bias=1.0), tanh_done[n],
                       tmp_read[b])
                l2[n] = A(lambda e, r, n=n: e.activation(TH[:, n, :], TH[:, n, :], ACT.Ln, scale=2.0, bias=tiny[:, 0:1]),
                          l1)
            for n in pair:
                b = n % 2
                tmp_read[b] = V(lambda e, r, n=n, b=b: e.tensor_tensor(TH[:, n, :], TH[:, n, :], G[b][:], ALU.subtract),
                                l2[n])
                m_[n] = A(lambda e, r, n=n: e.activation(TH[:, n, :], TH[:, n, :], ACT.Exp, scale=0.5), tmp_read[b])
            for n in pair:
                t_ = V(lambda e, r, n=n: e.memset(TH[:, n, 0:1], 1.0), m_[n])
                t_ = V(lambda e, r, n=n: e.tensor_tensor(XC[:, n, :], XC[:, n, :], TH[:, n, :], ALU.mult), t_, scan_in[n])
                mults.append(V(lambda e, r, n=n: e.tensor_tensor_scan(XC[:, n, :], LX[:, n, :], XC[:, n, :], 0.0,
                                                                      ALU.mult, ALU.add), t_, a_[n]))

        def branch_out(n):
            g_ = A(lambda e, r: e.activation(LG[:, n, :], LG[:, n, :], ACT.Gelu_apprx_tanh), lg[n])
            m_ = V(lambda e, r: e.tensor_tensor(XC[:, n, :], XC[:, n, :], LG[:, n, :], ALU.mult), g_, mults[n])
            hh = A(lambda e, r: e.activation(LXH[:, n, :], XC[:, n, :], ACT.Copy), m_)
            out_h.append(V(lambda e, r: e.tensor_tensor(LGL[:, n, :], XC[:, n, :], LXH[:, n, :].bitcast(F32),
                                                        ALU.subtract), hh))

        def pool_map():
            for g in range(4):
                t_ = TE(lambda e, r, g=g: e.matmul(ps[4 + g][:], pw[:, g, :], UP[:, g, :], start=True, stop=True),
                        pool_d[g], pw_in, gate_read[4 + g][0])
                hh = A(lambda e, r, g=g: e.activation(PH[:, g, :], ps[4 + g][:], ACT.Copy,
                                                      scale=scol("pool_scale_2")(g)), t_, bd_read)
                ph.append(V(lambda e, r, g=g: e.scalar_tensor_tensor(
                    out=UPL[:, g, :], in0=ps[4 + g][:], scalar=scol("pool_scale_2")(g), in1=PH[:, g, :].bitcast(F32),
                    op0=ALU.mult, op1=ALU.subtract), hh))

        mults, ph, out_h, gp, gr, r_ready = [], [], [], [], [], []

        def take_first(ends, r_m):
            r_ready.append(r_m)
            return take4(LX, 0)(ends, r_m)
        lx = in_group(0, take_first)
        r_sum = r_ready[0]
        conv4(0), conv4(1)
        lx += in_group(1, take4(LX, 4), lambda: lru_pair(0))
        conv4(2), conv4(3)
        up = in_group(2, take4(UP, 0), lambda: lru_pair(2))
        conv4(4), conv4(5)
        rest = pool(0)
        lg = in_group(3, take4(LG, 0), lambda: lru_pair(4))
        conv4(6), conv4(7)
        rest()
        rest = pool(1)
        lg += in_group(4, take4(LG, 4), lambda: lru_pair(6))
        bd_read = pr.now(s_t)
        rest()
        rest = pool(2)
        ln_exp_table()
        scan_pair(0)
        gz = in_group(5, take4(GP, 0))
        rest()
        rest = pool(3)
        scan_pair(2)
        scan_pair(4)
        gz += in_group(6, take4(GP, 4))
        rest()
        scan_pair(6)
        rz = in_group(7, take4(GR, 0, mults[-1]), pool_map)
        for n in range(4):
            branch_out(n)
        rz += in_group(8, take4(GR, 4))
        for n in range(4, 8):
            branch_out(n)
        gp = [A(lambda e, r, n=n: e.activation(GP[:, n, :], GP[:, n, :], ACT.Sigmoid), gz[n]) for n in range(DC)]
        ends = last_units(0, 4, lambda kc: (PH[:, kc, :], UPL[:, kc, :]), [[m_] for m_ in ph],
                          ev_waits() + [[m_] for m_ in ph])
        in_read = pr.now(s_mm)
        yp = [V(lambda e, r, n=n: e.tensor_tensor(GP[:, n, :], GP[:, n, :], ps[n][:], ALU.mult), ends[n // 2], gp[n])
              for n in range(DC)]
        for n in range(DC):
            gr.append(A(lambda e, r, n=n: e.activation(GR[:, n, :], GR[:, n, :], ACT.Sigmoid), rz[n]))
            if n < 4:
                ahead()
        for k in range(4):
            use_unit(full_unit(k, 8, lambda kc: (LXH[:, kc, :], LGL[:, kc, :]), [out_h[k]], [[y_] for y_ in yp]))
            ahead()
        ends = last_units(4, 8, lambda kc: (LXH[:, kc, :], LGL[:, kc, :]), [[m_] for m_ in out_h[4:8]])
        mh, yr = [], []

        def low_parts(n):
            mh.append(V(lambda e, r: e.tensor_tensor(HL[:, n, :], GR[:, n, :], HH[:, n, :].bitcast(F32), ALU.subtract),
                        merged[n]))
        merged = []
        for n0 in range(0, DC, 2):
            if n0 == 6:
                ahead()
            for n in (n0, n0 + 1):
                yr.append([V(lambda e, r, n=n: e.tensor_tensor(GR[:, n, :], GR[:, n, :], ps[n][:], ALU.mult),
                             ends[n // 2], gr[n])])
            for n in (n0, n0 + 1):
                m_ = V(lambda e, r, n=n: e.tensor_tensor(GR[:, n, :], GR[:, n, :], GP[:, n, :], ALU.add), *yr[n], yp[n])
                merged.append(A(lambda e, r, n=n: e.activation(HH[:, n, :], GR[:, n, :], ACT.Copy), m_, in_read))
            for n in (n0 - 2, n0 - 1) if n0 else ():
                low_parts(n)
        low_parts(6), low_parts(7)
        for _ in range(3):
            ahead()
        for k in range(4):
            use_unit(full_unit(k, 8, lambda kc: (HH[:, kc, :], HL[:, kc, :]), [mh[k]], yr))
            ahead()
        ends = last_units(4, 8, lambda kc: (HH[:, kc, :], HL[:, kc, :]), [[m_] for m_ in mh[4:8]])

        h, sq, evs, free = stage_end(ends, gu(0), scol("g_ffn_pre_2"), scol("g_mix_post_2"))
        CG = [at(f"CG{j}", [P, T], F32, rope_at + 2 * KB * j) for j in range(2)]
        fw_cols = sb("fw_cols", [P, 4, 2])
        cw0, cb0 = cs["ffn_conv_w_2"], cs["ffn_conv_b_2"]
        taps = par[:, cw0:cw0 + 72].rearrange("p (k c) -> p k c", k=3)

        def conv_gelu_chunk(g, ends, r_m, ahead):
            dyn = lambda r: ds(g(r) * 2, 2) if callable(g) else slice(2 * g, 2 * g + 2)
            dynb = lambda r: ds(g(r) * 2 + cb0, 2) if callable(g) else slice(cb0 + 2 * g, cb0 + 2 * g + 2)
            V(lambda e, r: e.tensor_copy(fw_cols[:, 0:3, :], taps[:, :, dyn(r)]), pr.now(s_d))
            V(lambda e, r: e.tensor_copy(fw_cols[:, 3, :], par[:, dynb(r)]), pr.now(s_d))
            s_ = []
            for j in range(2):
                gm = EV(lambda e, r, j=j: e.tensor_tensor(G[j][:], ps[2 * j][:], R[:], ALU.mult), ends[2 * j], r_m)
                um = EV(lambda e, r, j=j: e.tensor_tensor(U[j][:], ps[2 * j + 1][:], R[:], ALU.mult), ends[2 * j + 1])
                c_ = V(lambda e, r, j=j: e.tensor_scalar(CG[j][:], G[j][:], fw_cols[:, 2, j:j + 1],
                                                         fw_cols[:, 3, j:j + 1], ALU.mult, ALU.add), gm, pr.now(s_d))
                for k, sh in ((1, 1), (0, 2)):
                    c_ = V(lambda e, r, j=j, k=k, sh=sh: e.scalar_tensor_tensor(
                        out=CG[j][:, sh:T], in0=G[j][:, 0:T - sh], scalar=fw_cols[:, k, j:j + 1],
                        in1=CG[j][:, sh:T], op0=ALU.mult, op1=ALU.add), c_)
                s_.append((A(lambda e, r, j=j: e.activation(CG[j][:], CG[j][:], ACT.Gelu_apprx_tanh), c_), um))
            ahead()
            fs = [V(lambda e, r, j=j: e.tensor_tensor(U[j][:], U[j][:], CG[j][:], ALU.mult), *s_[j]) for j in range(2)]
            for j in range(2):
                hh = A(lambda e, r, j=j: e.activation(hid_slot(HIDHf, g, j)(r), U[j][:], ACT.Copy), fs[j])
                V(lambda e, r, j=j: e.tensor_tensor(hid_slot(HIDLf, g, j)(r), U[j][:],
                                                    hid_slot(HIDHf, g, j)(r).bitcast(F32), ALU.subtract), hh)

        dn = down_unit("w_down_2", FF2, None)
        early, late = swiglu_groups(h, sq, free, gu, FF2 // 256, conv_gelu_chunk, [dn(k) for k in range(4)],
                                    [evs[7]])
        pproj, gates = ple_units("w_ple_proj_2", "w_ple_gate_2", None)
        ple_u = pproj + gates
        ends = down(FF2 // P, 4, dn, [early], [late])
        eb = []

        def fill(evs, rp):
            p_in = dma(lambda e, r: e.dma_start(PTOK[:], a["p_2"][0, 0].rearrange("(t q) c -> q t c", q=P)), s_ptok,
                       ends[3])
            embeddings(p_in, 6, evs[6:8])
            return embedding_products([[m_, rp] for m_ in evs], eb)
        h, sq, evs, free = stage_end(ends, ple_u[0:6], scol("g_ple_gate_2"), scol("g_ffn_post_2"), fill=fill)
        ES = at("ES", [P, DC, T], F32, hid_at + 48 * KB)
        e_sum = None
        for n in range(DC):
            q_ = A(lambda e, r, n=n: e.activation(ES[:, n, :], E[:, n, :], ACT.Square), eb[n])
            if n:
                e_sum = G_(lambda e, r, n=n: e.tensor_tensor(ES[:, 0, :], ES[:, 0, :], ES[:, n, :], ALU.add), q_, e_sum)
        for kp in range(4):
            e_ = use_unit(group_unit((2 * kp, 2 * kp + 1), wat4, range(4), DC, (HH, HL), h, [[m_] for m_ in eb[0:4]]))
            if kp == 2:
                r_m = rms(R, 7, D, sq, eb[7])
            if kp < 3:
                fetch(ple_u[kp + 6])
        gate = []

        def gates_of(n, end):
            z_ = V(lambda e, r: e.tensor_tensor(Y[:, n, :], ps[n][:], R[:], ALU.mult), end, r_m)
            gate.append(A(lambda e, r: e.activation(Y[:, n, :], Y[:, n, :], ACT.Sigmoid), z_))
            return z_
        z_ = [gates_of(n, e_[n]) for n in range(4)]
        fetch(ple_u[9])
        re = rstd(U[1], 0, D, TE(lambda e, r: e.matmul(ps[0][:], ones, ES[:, 0, :], start=True, stop=True), e_sum,
                                 z_[0]))
        for n in range(DC):
            en = V(lambda e, r, n=n: e.scalar_tensor_tensor(out=E[:, n, :], in0=E[:, n, :],
                                                            scalar=scol("g_ple_post_2")(n), in1=U[1][:],
                                                            op0=ALU.mult, op1=ALU.mult), re)

        def gated_update(n):
            y_ = V(lambda e, r: e.tensor_tensor(Y[:, n, :], Y[:, n, :], E[:, n, :], ALU.mult), gate[n], en)
            return V(lambda e, r: e.tensor_tensor(X[:, n, :], X[:, n, :], Y[:, n, :], ALU.add), y_)
        x_out = [gated_update(n) for n in range(4)]
        e_ = gate_group(range(4, 8), [[eb[b], r_m] for b in range(4, 8)])
        for n in range(4, 8):
            gates_of(n, e_[n - 4])
            x_out.append(gated_update(n))
        o_evs = []
        otok = at("otok", [P, TC, D], F32, hid_at + 32 * KB)
        for half in range(2):
            for t in range(TC):
                for q in range(4):
                    n = half * 4 + q
                    (TE if q == 3 else mm)(
                        lambda e, r, t=t, q=q, n=n: e.transpose(ps[t][:, q * P:(q + 1) * P],
                                                                X[:, n, t * P:(t + 1) * P], ident),
                        x_out[n], *(o_evs[t:t + 1] if half else []))
                if half == 0:
                    o_evs.append(A(lambda e, r, t=t: e.activation(otok[:, t, 0:512], ps[t][:], ACT.Copy), pr.now(s_t)))
                else:
                    o_evs.append(V(lambda e, r, t=t: e.tensor_copy(otok[:, t, 512:1024], ps[t][:]), pr.now(s_t)))
                dma(lambda e, r, t=t, half=half: e.dma_start(out[0, t * P:(t + 1) * P, half * 512:(half + 1) * 512],
                                                             otok[:, t, half * 512:(half + 1) * 512]), s_out, o_evs[-1])
        all_out = pr.now(s_out)

        block = ctx.enter_context(nc.Block())

        @block.sync
        def _(e):
            pr.emit("sync", e)
            e.wait_ge(s_out.handle, all_out.value({}))

        @block.scalar
        def _(e):
            pr.emit("scalar", e)

        @block.vector
        def _(e):
            pr.emit("vector", e)

        @block.gpsimd
        def _(e):
            pr.emit("gpsimd", e)

        @block.tensor
        def _(e):
            pr.emit("tensor", e)


INPUTS = ("x", "p", "positions", "g_ffn1_pre", "w1_gate", "w1_up", "w1_down", "g_ffn1_post", "g_mix_pre", "w_in",
          "g_mla_q", "w_mla_uq", "g_mla_kv", "w_mla_ukv", "w_conv", "w_out", "g_mix_post", "g_ffn2_pre", "w2_gate",
          "w2_up", "w2_down", "g_ffn2_post", "g_ple_pre", "w_ple_gate", "w_ple_proj", "g_ple_post", "p_2",
          "g_mix_pre_2", "g_mix_post_2", "w_in_2", "pool_w_2", "pool_scale_2", "w_pool_out_2", "conv_w_2", "conv_b_2",
          "w_rg_gates_2", "b_rg_gates_2", "lru_lambda_2", "w_rg_out_2", "w_o_2", "g_ffn_pre_2", "g_ffn_post_2",
          "w_up_2", "ffn_conv_w_2", "ffn_conv_b_2", "w_down_2", "g_ple_gate_2", "w_ple_gate_2", "w_ple_proj_2",
          "g_ple_post_2")


def constant_table():
    row, col = np.arange(P)[:, None], np.arange(P)[None, :]
    c = np.zeros((P, CONSTS), np.float32)
    c[:, 0:P] = row == col
    c[:, P:2 * P] = 1
    c[:, 2 * P:3 * P] = -1
    c[:, 3 * P:4 * P] = np.where(row >= col, -1, 0)
    c[:, 4 * P:5 * P] = row < col
    c[:, 5 * P:6 * P] = np.where(row < col, 0, NEG_INF)
    c[:, 6 * P:7 * P] = np.where(col <= row, 0, NEG_INF)
    half = ROPE // 2
    freq = np.float32(ROPE_BASE) ** (-np.arange(half, dtype=np.float32) / np.float32(half))
    for m in range(P):
        if m % ROPE < half:
            c[m + half, 7 * P + m] = -1
        else:
            c[m - half, 7 * P + m] = 1
        c[m, 8 * P] = freq[m % half]
    c[:, 8 * P + 1:] = 1.0 / np.arange(1, 17, dtype=np.float32)
    return c


def kernel(**inputs):
    import concourse.bacc as bacc
    from concourse.bass_utils import run_bass_kernel_spmd

    nc = bacc.Bacc("TRN2", target_bir_lowering=False, num_devices=1)
    arrays, aps = {}, {}
    for name in INPUTS:
        v = np.ascontiguousarray(inputs[name])
        arrays[f"in_{name}"] = v
        aps[name] = nc.dram_tensor(f"in_{name}", v.shape, mybir.dt.from_np(v.dtype), kind="ExternalInput").ap()
    arrays["in_constants"] = constant_table()
    consts_dram = nc.dram_tensor("in_constants", (P, CONSTS), F32, kind="ExternalInput").ap()
    out = nc.dram_tensor("out_x", (1, T, D), F32, kind="ExternalOutput").ap()
    build_program(nc, aps, consts_dram, out)
    return run_bass_kernel_spmd(nc, [arrays], core_ids=[0]).results[0]["out_x"]
```
